# Optimizing a Trainium2 kernel written in Bass

```python
import jax, jax.numpy as jnp
from jax import lax
import numpy as np

D_MODEL = 1024
BATCH = 1
SEQ = 512
DEPTH = 2

D_MIX = D_MODEL
NSA_HEADS = 6
NSA_KV_HEADS = 2
NSA_HPG = NSA_HEADS // NSA_KV_HEADS
NSA_DH = 64
NSA_CMP_LEN = 32
NSA_CMP_STRIDE = 16
NSA_SLC_LEN = 64
NSA_TOPN = 16
NSA_WINDOW = 512
NSA_Q_BLOCK = 64
NSA_FORCE = 1.0e4
MLA_HEADS = 6
MLA_Q_LORA = 256
MLA_KV_LORA = 128
MLA_NOPE = 64
MLA_ROPE = 32
MLA_VDIM = 64
MLA_Q_BLOCK = 128
ROPE_THETA = 10000.0
POOL_WINDOWS = (2, 4, 8, 16)
POOL_GROUP = 64
POOL_WIDTH = 4 * POOL_GROUP
D_FF = 4 * D_MODEL
EPS = 1e-6

NSA_Q_W = NSA_HEADS * NSA_DH
NSA_KV_W = 3 * 2 * NSA_KV_HEADS * NSA_DH
NSA_GATE_W = 3 * NSA_HEADS
IN_SPLITS = (NSA_Q_W, NSA_KV_W, NSA_GATE_W, MLA_Q_LORA, MLA_KV_LORA, MLA_ROPE, POOL_WIDTH)
P_IN = 384 + 768 + 18 + 256 + 128 + 32 + 256

kernel_name = 'hybrid_nsa_mla_pool_trunk'

def rmsnorm(x, g):
    x32 = x.astype(jnp.float32)
    y = x32 * lax.rsqrt(jnp.mean(x32 * x32, axis=-1, keepdims=True) + EPS)
    return (y * g.astype(jnp.float32)).astype(x.dtype)

def masked_softmax(s, mask):
    s = jnp.where(mask, s.astype(jnp.float32), -jnp.inf)
    m = jnp.max(s, axis=-1, keepdims=True)
    m = jnp.where(jnp.isfinite(m), m, 0.0)
    e = jnp.exp(s - m)
    d = jnp.sum(e, axis=-1, keepdims=True)
    return e / jnp.maximum(d, jnp.finfo(jnp.float32).tiny)

def rope_cos_sin(positions, dim):
    half = dim // 2
    inv = jnp.power(jnp.float32(ROPE_THETA), -(jnp.arange(half, dtype=jnp.float32) / half))
    ang = positions.astype(jnp.float32)[..., None] * inv
    return jnp.cos(ang), jnp.sin(ang)

def apply_rope(x, cos, sin):
    half = x.shape[-1] // 2
    x1, x2 = x[..., :half], x[..., half:]
    cos = cos.astype(x.dtype)
    sin = sin.astype(x.dtype)
    return jnp.concatenate([x1 * cos - x2 * sin, x2 * cos + x1 * sin], axis=-1)

def nsa_compress(t, pos, w1, w2):
    B, G, T, DH = t.shape
    n_chunks = T // NSA_CMP_STRIDE
    r = NSA_CMP_LEN // NSA_CMP_STRIDE
    c = t.reshape(B, G, n_chunks, NSA_CMP_STRIDE, DH)
    blocks = jnp.concatenate([c[:, :, i:n_chunks - r + 1 + i] for i in range(r)], axis=3)
    h = jax.nn.gelu(jnp.einsum('bgnld,lde->bgne', blocks + pos, w1))
    return jnp.einsum('bgne,ef->bgnf', h, w2)

def cmp_to_slc_overlap(n_cmp, n_slc):
    start = np.arange(n_cmp)[:, None] * NSA_CMP_STRIDE
    end = start + NSA_CMP_LEN
    s0 = np.arange(n_slc)[None, :] * NSA_SLC_LEN
    s1 = s0 + NSA_SLC_LEN
    ov = np.clip(np.minimum(end, s1) - np.maximum(start, s0), 0, None) / NSA_CMP_LEN
    return jnp.asarray(ov, dtype=jnp.float32)

def nsa_mixer(q, kv, gate, cmp_pos, cmp_w1, cmp_w2):
    B, T, _ = q.shape
    G, HPG, DH = NSA_KV_HEADS, NSA_HPG, NSA_DH
    q = q.reshape(B, T, G, HPG, DH).transpose(0, 2, 3, 1, 4)
    kv = kv.reshape(B, T, 3, 2, G, DH).transpose(2, 3, 0, 4, 1, 5)
    g = jax.nn.sigmoid(gate).reshape(B, T, G, HPG, 3).transpose(0, 2, 3, 1, 4)

    k_cmp = nsa_compress(kv[0, 0], cmp_pos[0], cmp_w1[0], cmp_w2[0])
    v_cmp = nsa_compress(kv[0, 1], cmp_pos[1], cmp_w1[1], cmp_w2[1])
    n_cmp = k_cmp.shape[2]
    n_slc = T // NSA_SLC_LEN
    n_sel = min(NSA_TOPN, n_slc)
    overlap = cmp_to_slc_overlap(n_cmp, n_slc)
    k_blk = kv[1, 0].reshape(B, G, n_slc, NSA_SLC_LEN, DH)
    v_blk = kv[1, 1].reshape(B, G, n_slc, NSA_SLC_LEN, DH)
    pad = ((0, 0), (0, 0), (NSA_WINDOW, 0), (0, 0))
    k_win = jnp.pad(kv[2, 0], pad)
    v_win = jnp.pad(kv[2, 1], pad)

    cmp_end = jnp.arange(n_cmp) * NSA_CMP_STRIDE + NSA_CMP_LEN - 1
    blk_ids = jnp.arange(n_slc)
    scale = DH ** -0.5
    gather = jax.vmap(jax.vmap(lambda blocks, ix: blocks[ix]))

    def block_fn(c):
        q0 = c * NSA_Q_BLOCK
        qc = lax.dynamic_slice_in_dim(q, q0, NSA_Q_BLOCK, axis=3)
        gc = lax.dynamic_slice_in_dim(g, q0, NSA_Q_BLOCK, axis=3)
        qpos = q0 + jnp.arange(NSA_Q_BLOCK)
        s = jnp.einsum('bghqd,bgnd->bghqn', qc, k_cmp) * scale
        p_cmp = masked_softmax(s, cmp_end[None, :] <= qpos[:, None])
        o_cmp = jnp.einsum('bghqn,bgnd->bghqd', p_cmp.astype(v_cmp.dtype), v_cmp)
        imp = jnp.einsum('bghqn,ns->bgqs', p_cmp, overlap)
        cur = (qpos // NSA_SLC_LEN)[:, None]
        forced = (blk_ids[None, :] == 0) | (blk_ids[None, :] == cur) | (blk_ids[None, :] == cur - 1)
        valid = blk_ids[None, :] * NSA_SLC_LEN <= qpos[:, None]
        score = jnp.where(forced, NSA_FORCE, jnp.where(valid, imp, -1.0))
        _, idx = lax.top_k(score, n_sel)
        ks = gather(k_blk, idx).reshape(B, G, NSA_Q_BLOCK, n_sel * NSA_SLC_LEN, DH)
        vs = gather(v_blk, idx).reshape(B, G, NSA_Q_BLOCK, n_sel * NSA_SLC_LEN, DH)
        kpos = (idx[..., None] * NSA_SLC_LEN + jnp.arange(NSA_SLC_LEN)).reshape(B, G, NSA_Q_BLOCK, n_sel * NSA_SLC_LEN)
        s = jnp.einsum('bghqd,bgqkd->bghqk', qc, ks) * scale
        p = masked_softmax(s, (kpos <= qpos[:, None])[:, :, None])
        o_slc = jnp.einsum('bghqk,bgqkd->bghqd', p.astype(vs.dtype), vs)
        kw = lax.dynamic_slice_in_dim(k_win, q0, NSA_Q_BLOCK + NSA_WINDOW, axis=2)
        vw = lax.dynamic_slice_in_dim(v_win, q0, NSA_Q_BLOCK + NSA_WINDOW, axis=2)
        wpos = q0 - NSA_WINDOW + jnp.arange(NSA_Q_BLOCK + NSA_WINDOW)
        dist = qpos[:, None] - wpos[None, :]
        mask_w = (dist >= 0) & (dist < NSA_WINDOW) & (wpos[None, :] >= 0)
        s = jnp.einsum('bghqd,bgkd->bghqk', qc, kw) * scale
        p = masked_softmax(s, mask_w)
        o_win = jnp.einsum('bghqk,bgkd->bghqd', p.astype(vw.dtype), vw)
        return gc[..., 0:1] * o_cmp + gc[..., 1:2] * o_slc + gc[..., 2:3] * o_win

    o = lax.map(block_fn, jnp.arange(T // NSA_Q_BLOCK))
    return o.transpose(1, 0, 4, 2, 3, 5).reshape(B, T, NSA_HEADS * DH)

def mla_mixer(cq, ckv, k_rope, positions, q_norm_g, w_qup, kv_norm_g, w_kvup):
    B, T, _ = cq.shape
    q = (rmsnorm(cq, q_norm_g) @ w_qup).reshape(B, T, MLA_HEADS, MLA_NOPE + MLA_ROPE)
    kv = (rmsnorm(ckv, kv_norm_g) @ w_kvup).reshape(B, T, MLA_HEADS, MLA_NOPE + MLA_VDIM)
    cos, sin = rope_cos_sin(positions, MLA_ROPE)
    q_rope = apply_rope(q[..., MLA_NOPE:], cos[:, :, None], sin[:, :, None])
    k_rope = apply_rope(k_rope, cos, sin)
    q = jnp.concatenate([q[..., :MLA_NOPE], q_rope], axis=-1).transpose(0, 2, 1, 3)
    k = jnp.concatenate([kv[..., :MLA_NOPE],
                         jnp.broadcast_to(k_rope[:, :, None, :], (B, T, MLA_HEADS, MLA_ROPE))],
                        axis=-1).transpose(0, 2, 1, 3)
    v = kv[..., MLA_NOPE:].transpose(0, 2, 1, 3)
    scale = (MLA_NOPE + MLA_ROPE) ** -0.5
    kpos = jnp.arange(T)

    def block_fn(c):
        q0 = c * MLA_Q_BLOCK
        qc = lax.dynamic_slice_in_dim(q, q0, MLA_Q_BLOCK, axis=2)
        qpos = q0 + jnp.arange(MLA_Q_BLOCK)
        s = jnp.einsum('bhqd,bhkd->bhqk', qc, k).astype(jnp.float32) * scale
        s = jnp.where(kpos[None, :] <= qpos[:, None], s, -jnp.inf)
        p = jax.nn.softmax(s, axis=-1)
        return jnp.einsum('bhqk,bhkd->bhqd', p.astype(v.dtype), v)

    o = lax.map(block_fn, jnp.arange(T // MLA_Q_BLOCK))
    return o.transpose(1, 0, 3, 2, 4).reshape(B, T, MLA_HEADS * MLA_VDIM)

def pool_mixer(u, w_pool, scale):
    B, T, _ = u.shape
    u32 = u.astype(jnp.float32)
    csum = jnp.pad(jnp.cumsum(u32, axis=1), ((0, 0), (1, 0), (0, 0)))
    t_idx = jnp.arange(T)
    means = []
    for gi, w in enumerate(POOL_WINDOWS):
        cg = csum[..., gi * POOL_GROUP:(gi + 1) * POOL_GROUP]
        upper = cg[:, 1:T + 1]
        lower = jnp.pad(cg, ((0, 0), (w, 0), (0, 0)))[:, 1:T + 1]
        cnt = jnp.minimum(t_idx + 1, w).astype(jnp.float32)[None, :, None]
        means.append((upper - lower) / cnt)
    pooled = (jnp.concatenate(means, axis=-1) - u32).astype(u.dtype)
    pooled = pooled.reshape(B, T, len(POOL_WINDOWS), POOL_GROUP)
    y = jnp.einsum('btgc,gcd->btgd', pooled, w_pool).reshape(B, T, POOL_WIDTH)
    return y * scale

def setup_inputs(seed: int = 0) -> dict:
    key = jax.random.key(seed)
    ks = jax.random.split(key, 20)
    f32 = jnp.float32

    def nrm(k, shape, s):
        return jax.random.normal(k, shape, f32) * s

    x = jax.random.normal(ks[0], (BATCH, SEQ, D_MODEL), f32)
    positions = (jnp.arange(SEQ, dtype=jnp.int32)[None, :]
                 + jax.random.randint(ks[1], (BATCH, 1), 0, 1024, dtype=jnp.int32))
    return {
        'x': x,
        'positions': positions,
        'ln1_g': 1.0 + nrm(ks[2], (DEPTH, D_MODEL), 0.05),
        'w_in': nrm(ks[3], (DEPTH, D_MODEL, P_IN), D_MODEL ** -0.5),
        'nsa_cmp_pos': nrm(ks[4], (DEPTH, 2, NSA_CMP_LEN, NSA_DH), 0.1),
        'nsa_cmp_w1': nrm(ks[5], (DEPTH, 2, NSA_CMP_LEN, NSA_DH, NSA_DH), (NSA_CMP_LEN * NSA_DH) ** -0.5),
        'nsa_cmp_w2': nrm(ks[6], (DEPTH, 2, NSA_DH, NSA_DH), NSA_DH ** -0.5),
        'mla_q_norm': 1.0 + nrm(ks[7], (DEPTH, MLA_Q_LORA), 0.05),
        'mla_w_qup': nrm(ks[8], (DEPTH, MLA_Q_LORA, MLA_HEADS * (MLA_NOPE + MLA_ROPE)), MLA_Q_LORA ** -0.5),
        'mla_kv_norm': 1.0 + nrm(ks[9], (DEPTH, MLA_KV_LORA), 0.05),
        'mla_w_kvup': nrm(ks[10], (DEPTH, MLA_KV_LORA, MLA_HEADS * (MLA_NOPE + MLA_VDIM)), MLA_KV_LORA ** -0.5),
        'pool_w': nrm(ks[11], (DEPTH, len(POOL_WINDOWS), POOL_GROUP, POOL_GROUP), POOL_GROUP ** -0.5),
        'pool_scale': 1.0 + nrm(ks[12], (DEPTH, POOL_WIDTH), 0.1),
        'w_out': nrm(ks[13], (DEPTH, D_MIX, D_MODEL), D_MIX ** -0.5),
        'ln2_g': 1.0 + nrm(ks[14], (DEPTH, D_MODEL), 0.05),
        'w_ff1': nrm(ks[15], (DEPTH, D_MODEL, D_FF), D_MODEL ** -0.5),
        'w_ff2': nrm(ks[16], (DEPTH, D_FF, D_MODEL), D_FF ** -0.5),
        'final_g': 1.0 + nrm(ks[17], (D_MODEL,), 0.05),
    }

def reference(x, positions, ln1_g, w_in, nsa_cmp_pos, nsa_cmp_w1, nsa_cmp_w2, mla_q_norm, mla_w_qup,
              mla_kv_norm, mla_w_kvup, pool_w, pool_scale, w_out, ln2_g, w_ff1, w_ff2, final_g):
    offsets = np.cumsum(IN_SPLITS)[:-1].tolist()
    for l in range(DEPTH):
        h = rmsnorm(x, ln1_g[l])
        z = h @ w_in[l]
        nq, nkv, ngate, cq, ckv, kr, pu = jnp.split(z, offsets, axis=-1)
        o_nsa = nsa_mixer(nq, nkv, ngate, nsa_cmp_pos[l], nsa_cmp_w1[l], nsa_cmp_w2[l])
        o_mla = mla_mixer(cq, ckv, kr, positions, mla_q_norm[l], mla_w_qup[l], mla_kv_norm[l], mla_w_kvup[l])
        o_pool = pool_mixer(pu, pool_w[l], pool_scale[l])
        mix = jnp.concatenate([o_nsa, o_mla, o_pool], axis=-1)
        x = x + mix @ w_out[l]
        h = rmsnorm(x, ln2_g[l])
        x = x + jnp.square(jax.nn.relu(h @ w_ff1[l])) @ w_ff2[l]
    return rmsnorm(x, final_g)


_drawn_inputs = setup_inputs


def setup_inputs(seed=0):
    import zlib

    import numpy as np

    out = dict(_drawn_inputs(seed))
    spreads = {}
    factors = {'mla_q_norm': 8.0, 'mla_kv_norm': 5.174}
    for name, (base, spread) in spreads.items():
        noise = np.random.default_rng([zlib.crc32(name.encode()), seed]).standard_normal(out[name].shape)
        drawn = base * np.exp(spread * noise) if base else spread * noise
        out[name] = __import__('jax').numpy.asarray(drawn.astype(out[name].dtype))
    for name, factor in factors.items():
        out[name] = (out[name] * factor).astype(out[name].dtype)
    return out
```

```python
from contextlib import ExitStack

import numpy as np

import concourse.bass as bass
from concourse import mybir

ALU = mybir.AluOpType
ACT = mybir.ActivationFunctionType
AX_X = mybir.AxisListType.X
F32 = mybir.dt.float32
F32R = mybir.dt.float32r
BF16 = mybir.dt.bfloat16
I32 = mybir.dt.int32

P = 128
T = 512
TT = T // P
D = 1024
KT = D // P
DEPTH = 2
EPS = 1e-6
NEG = -1.0e30
NEG_GUARD = -1.0e29
TINY = float(np.finfo(np.float32).tiny)

NSA_H, NSA_G, NSA_HPG, DH = 6, 2, 3, 64
CMP_LEN, CMP_STRIDE, NB = 32, 16, 32
GATE_W = 3 * NSA_H
MLA_H, NOPE, ROPE, VD = 6, 64, 32, 64
QK = NOPE + ROPE
Q_LORA, KV_LORA = 256, 128
POOL_G = 64
D_FF = 4 * D
CHUNKS = 4

C_Q, C_KV, C_GATE, C_CQ, C_CKV, C_KR, C_POOL = 0, 384, 1152, 1170, 1426, 1554, 1586

IN_UNITS = [
    [(C_CQ, 256)],
    [(C_CKV, 160)],
    [(C_KV, 256)],
    [(C_KV + 256, 128), (C_KV + 512, 128)],
    [(C_KV + 384, 128), (C_KV + 640, 128)],
    [(C_Q, 256)],
    [(C_Q + 256, 128)],
    [(C_POOL, 256)],
]
IN_WIDTH = [256, 256, 256, 256, 256, 256, 128, 256]
X_PIECES = 4
U_OUT = len(IN_UNITS)
U_FF = U_OUT + 4
UNITS = U_FF + 8 * CHUNKS

JOBS = [("cq0", 0), ("cq1", 1), ("ncol", 7), ("post", 6), ("ckv", 2), ("nbc", 6), ("kr", 3),
        ("kc", 0), ("vc", 1), ("mcol", 7), ("ks", 2), ("kw", 3), ("mbq", 6), ("mbk", 7),
        ("v0", 0), ("v1", 1), ("v2", 2), ("v3", 3), ("q0", 0), ("q1", 1), ("hk", 4), ("hv", 5),
        ("q2", 2), ("u0", 3), ("u1", 0),
        ("uq0", 1), ("uq1", 2), ("k2", 4), ("w2", 5), ("uq2", 3), ("uq3", 0), ("py0", 4), ("py1", 5),
        ("cs0", 6), ("cs1", 7), ("uq4", 1), ("uq5", 2), ("kn0", 3), ("kn1", 0), ("kn2", 1),
        ("vm0", 2), ("vm1", 3), ("vm2", 0), ("vm3", 1)]
N_UNITS_ATT = 2 * NSA_H + MLA_H
PAIR_OF = {}
for _h in range(NSA_H):
    PAIR_OF[2 * _h] = PAIR_OF[2 * _h + 1] = _h // 2
for _h in range(MLA_H):
    PAIR_OF[2 * NSA_H + _h] = NSA_H // 2 + _h // 2
for _s in range(N_UNITS_ATT + 2):
    if _s < N_UNITS_ATT:
        JOBS += [(f"s{_s}a", 0), (f"s{_s}b", 1), (f"s{_s}c", 2)]
    if _s == 0:
        JOBS += [("ct0", 4), ("ct1", 5)]
    if 1 <= _s <= N_UNITS_ATT:
        JOBS += [(f"t{_s - 1}a", 3), (f"t{_s - 1}b", 4), (f"t{_s - 1}c", 5)]
    if _s >= 2 and (_s == 2 or PAIR_OF[_s - 2] != PAIR_OF[_s - 3]):
        JOBS += [(f"o{PAIR_OF[_s - 2]}", 6 + PAIR_OF[_s - 2] % 2)]
JOBS += [(f"x{m}", m % 4) for m in range(KT)]
JOBS += [("ncol2", 7), ("nbc2", 6)]
FF_JOBS = [(f"f{m}", m % 4) for m in range(KT)] + [(f"g{m}", m % 4) for m in range(KT)]
PRE_JOBS = [("par", 7)] + [(f"p{m}", m % 7) for m in range(KT)]
POST_JOBS = [("ncol3", 7)] + [(f"y{n}", n) for n in range(2 * TT)]

PAR0 = KT
PAR_L = 2 * KT + 5
G_LN2, G_NEXT, G_QN, G_KVN, G_PS = 0, KT, 2 * KT, 2 * KT + 2, 2 * KT + 3

K_ID, K_CM, K_RC, K_INVW, K_INVF, K_SIGN, K_ONE = 0, 128, 256, 288, 290, 291, 292
K_W = 293

S_TILES = [(3, 0, 0, 0), (2, 1, 0, 512), (0, 1, 384, 896), (1, 2, 0, 1024)]
S_PSUM = {i: c for i, _, c, _ in S_TILES}
S_COL = {i: c for i, _, _, c in S_TILES}
T_TILES = [(0, 0, 0, 0), (1, 1, 0, 512), (3, 1, 384, 896), (2, 2, 0, 1024)]
T_COL = {j: c for j, _, _, c in T_TILES}
PW = 1280


def bank_counts(jobs):
    return [sum(b == k for _, b in jobs) for k in range(8)]


class Psum:

    def __init__(self):
        self.pre, self.body = bank_counts(PRE_JOBS), bank_counts(JOBS)
        self.ff = bank_counts(FF_JOBS)
        self.layer = [a + CHUNKS * f for a, f in zip(self.body, self.ff)]
        self.place = {}
        for jobs, base, kind in ((PRE_JOBS, [0] * 8, "pre"), (JOBS, self.pre, "layer"),
                                 (FF_JOBS, [a + b for a, b in zip(self.pre, self.body)], "ff"),
                                 (POST_JOBS, [a + DEPTH * b for a, b in zip(self.pre, self.layer)], "post")):
            seen = list(base)
            for name, b in jobs:
                self.place[name] = (b, seen[b], kind)
                seen[b] += 1

    def bank(self, name):
        return self.place[name][0]

    def before(self, name, l=0, c=0):
        b, n, kind = self.place[name]
        if kind in ("pre", "post"):
            return n
        v = l * self.layer[b] + n
        return v + c * self.ff[b] if kind == "ff" else v


PS = Psum()


class Chain:

    def __init__(self, eng, sem, per_layer, base=0):
        self.eng, self.sem, self.per, self.base, self.n, self.l = eng, sem, per_layer, base, 0, 0

    def layer(self, l):
        self.n, self.l = 0, l

    def link(self, ins):
        ins.then_inc(self.sem, 1)
        self.n += 1
        self.eng.wait_ge(self.sem, self.l * self.per + self.base + self.n)


def build(nc, x, positions, ln1_g, w_in, nsa_cmp_pos, nsa_cmp_w1, nsa_cmp_w2, mla_q_norm, mla_w_qup,
          mla_kv_norm, mla_w_kvup, pool_w, pool_scale, w_out, ln2_g, w_ff1, w_ff2, final_g,
          consts, tri, out):
    with ExitStack() as ctx:
        top = [-(-nc.sbuf_base // 32) * 32]

        def at_(name, shape, dt, offset):
            return nc.alloc_sbuf_tensor_at(name, shape, dt, offset=offset)

        def size(shape, dt):
            return int(np.prod(shape[1:])) * (2 if dt == BF16 else 4)

        def sb(name, shape, dt=F32):
            t = at_(name, shape, dt, top[0])
            t_off[name] = top[0]
            top[0] += -(-size(shape, dt) // 32) * 32
            return t

        t_off = {}

        def sem(name):
            return ctx.enter_context(nc.semaphore(name))

        xT = sb("xT", [P, KT, T])
        XH, XL = sb("XH", [P, KT, T], F32R), sb("XL", [P, KT, T], F32R)
        BH, BL = sb("BH", [P, KT, T], F32R), sb("BL", [P, KT, T], F32R)
        raw = sb("raw", [P, 2, KT, 256])
        WH, WL = sb("WH", [P, 2, KT, 256], F32R), sb("WL", [P, 2, KT, 256], F32R)
        io = sb("io", [P, TT, D])
        PT = sb("PT", [P, 2, PW])
        rs = sb("rs", [P, T])
        sqt = sb("sqt", [P, 3, T])
        costab, sintab = sb("costab", [P, T]), sb("sintab", [P, T])
        ct = sb("ct", [P, K_W])
        identb, trib = sb("identb", [P, P], BF16), sb("trib", [P, P], BF16)
        qT = sb("qT", [P, 3, T])
        KSH = sb("KSH", [P, 2, 2, T], F32R)
        VN = sb("VN", [P, TT, 256])
        gz, gates = sb("gz", [P, TT, GATE_W]), sb("gates", [P, TT, GATE_W])
        cq, ckv = sb("cq", [P, 2, T]), sb("ckv", [P, T])
        kcv = sb("kcv", [P, 2, T + CMP_STRIDE])
        up = sb("up", [P, 2, T + CMP_STRIDE])
        PTc = sb("PTc", [P, 2, T])
        kc2, vcr = sb("kc2", [P, 2 * NB]), sb("vcr", [P, 2, DH])
        pos2 = sb("pos2", [P, 2 * CMP_LEN])
        pw = sb("pw", [P, 2, P])
        params, gl = sb("params", [P, PAR0 + DEPTH * PAR_L]), sb("gl", [P, PAR_L])
        graw = sb("graw", [P, KT, GATE_W])
        rcol = sb("rcol", [P, 12])
        na, nt, ni = sb("na", [P, 8]), sb("nt", [P, 8]), sb("ni", [P, 8], I32)
        nmax, nms = sb("nmax", [P, 2, TT]), sb("nms", [P, 2, TT])
        ssum, fac = sb("ssum", [P, 2, TT]), sb("fac", [P, 2, TT])
        cmx, csm = sb("cmx", [P, 4 * NSA_H]), sb("csm", [P, 4 * NSA_H])
        assert top[0] <= nc.sbuf_usable_end, (top[0], nc.sbuf_usable_end)

        def over(name, shape, dt, host, skip=0):
            return at_(name, shape, dt, t_off[host] + skip)

        QM = over("QM", [P, MLA_H, T], F32, "XH")
        KM = over("KM", [P, MLA_H, T], F32, "XL")
        wq = over("wq", [P, 2, MLA_H, P], F32, "BH")
        wkv = over("wkv", [P, 2, MLA_H, 64], F32, "BH", 6144)
        w2 = over("w2", [DH, 3, DH], F32, "BH", 9216)
        KSL = [over(f"KSL{b}", [P, 2, T], F32R, t, 6 * T * 4) for b, t in enumerate(("XH", "XL"))]
        QS = [over(f"QS{h}", [P, T], F32R, "BL", h * T * 4) for h in range(4)] +\
             [over(f"QS{h}", [P, T], F32R, "BH", (h - 2) * T * 4) for h in range(4, NSA_H)]
        kraw = over("kraw", [P, 2, T], F32, "io", 10240)
        bcmp = over("bcmp", [P, 2, 16, 2 * NB], F32, "BL")
        sc = over("sc", [P, TT, NSA_H, NB], F32, "BL", 8192)
        hx, hg = (over(n, [DH, 2, 2 * NB], F32, "BL", 11264 + 512 * k) for k, n in enumerate(["hx", "hg"]))
        pr = over("pr", [P, 2, PW], F32, "io")
        VM = over("VM", [P, TT, MLA_H * VD], F32, "io", 10240)
        pa, pb = (over(n, [P, 2, T + CMP_STRIDE], F32, "io", k * 4224) for k, n in enumerate(["pa", "pb"]))
        prs = over("prs", [2 * CMP_LEN, P], F32, "io", 9024)
        w1 = over("w1", [P, 2, 16, DH], F32, "PT")
        GH = over("GH", [P, KT, GATE_W], F32R, "PT", 8192)
        GL = over("GL", [P, KT, GATE_W], F32R, "PT", 8192 + 576)
        krz, krt = over("krz", [P, T], F32, "PTc"), over("krt", [P, T], F32, "PTc", 2048)
        relu, asq = (over(n, [P, 2, T], F32, "io", k * 4096) for k, n in enumerate(["relu", "asq"]))
        prow = over("prow", [P, P], F32, "sqt")
        trif = over("trif", [P, P], F32, "sqt", 512)
        posi = over("posi", [P, T], I32, "KSH")
        trig = over("trig", [P, 3, T], F32, "KSH", 2048)
        identr = over("identr", [P, P], F32R, "KSH")
        ident = ct[:, K_ID:K_ID + P]
        ones = ct[:, K_ONE:K_ONE + 1]

        psum = ctx.enter_context(nc.psum_tensor("psum", [P, 8, 512], F32))

        def f32(ap):
            return ap.bitcast(F32)

        def rot(h):
            if h % 2:
                return up[64:96, 0, CMP_STRIDE:], up[64:96, 1, CMP_STRIDE:]
            return kcv[64:96, 0, 0:T], kcv[64:96, 1, 0:T]

        full = [sem(f"bank_full{b}") for b in range(8)]
        moved = [sem(f"bank_moved{b}") for b in range(8)]
        x_loaded = [sem(f"x_loaded{k}") for k in range(X_PIECES)]
        par_loaded, const_loaded = sem("par_loaded"), sem("const_loaded")
        small_loaded, gate_loaded = sem("small_loaded"), sem("gate_loaded")
        raw_loaded = [sem(f"raw_loaded{s}") for s in range(2)]
        w_lo0 = sem("w_lo0")
        w_hi, w_lo = sem("w_hi"), sem("w_lo")
        kr_cols = sem("kr_cols")
        wq_cols = sem("wq_cols")
        zeros_set, pads_set, masks_set = sem("zeros_set"), sem("pads_set"), sem("masks_set")
        gl_ready = sem("gl_ready")
        xh_ready, xl_ready = sem("xh_ready"), sem("xl_ready")
        sq_ready, sq_added = sem("sq_ready"), sem("sq_added")
        rcol_ready, diag_ready, rb_ready = sem("rcol_ready"), sem("diag_ready"), sem("rb_ready")
        msq_ready, mdiag_ready = sem("msq_ready"), sem("mdiag_ready")
        kh_ready, kl_ready = sem("kh_ready"), sem("kl_ready")
        qh_ready, ql_ready = sem("qh_ready"), sem("ql_ready")
        gexp_ready, gates_ready = sem("gexp_ready"), sem("gates_ready")
        krot_ready, kr_spread = sem("krot_ready"), sem("kr_spread")
        bcmp_ready = sem("bcmp_ready")
        gelu_arg, gelu_exp, hg_ready = sem("gelu_arg"), sem("gelu_exp"), sem("hg_ready")
        pool_add, pooled_ready = sem("pool_add"), sem("pooled_ready")
        qrot_ready, qm_ready = sem("qrot_ready"), sem("qm_ready")
        csub_ready, cexp_ready, cp_ready = sem("csub_ready"), sem("cexp_ready"), sem("cp_ready")
        max_ready, fac_ready, p_ready = sem("max_ready"), sem("fac_ready"), sem("p_ready")
        bh_ready = sem("bh_ready")
        bl_ready = sem("bl_ready")
        asq_ready = sem("asq_ready")
        dve_step, pool_step = sem("dve_step"), sem("pool_step")
        trig_arg, sin_ready, trig_ready = sem("trig_arg"), sem("sin_ready"), sem("trig_ready")
        identr_ready, y_act, y_dve, stored = sem("identr_ready"), sem("y_act"), sem("y_dve"), sem("stored")

        def plain_waits(eng, *waits):
            values = [(s, eng.to_reg(v)) for s, v in waits]
            eng.wait_ge(const_loaded, 48)
            for s, v in values:
                eng.wait_ge(s, v)

        def free_before(name, l):
            return moved[PS.bank(name)], PS.before(name, l)

        def wait_full(eng, name, l=0, c=0):
            eng.wait_ge(full[PS.bank(name)], PS.before(name, l, c) + 1)

        def wait_moved(eng, name, l=0, c=0):
            eng.wait_ge(moved[PS.bank(name)], PS.before(name, l, c) + 1)

        def release(ins, name):
            ins.then_inc(moved[PS.bank(name)], 1)

        B_PL = KT + KT * CHUNKS
        B_ORDER = [6, 7, 0, 1, 2, 3, 4, 5]
        NSMALL = 15
        DVE_PRE, DVE_PL = 19, 99
        POOL_PRE, POOL_PL = 0, 5

        def split_counts(n, l, c=0):
            hi, lo = (1, 1) if n < 0 else (n + 3, n + 2)
            return (w_hi, l * HI_PL + c * 8 + hi), (w_lo, l * UNITS + c * 8 + lo)

        HI_PL = UNITS + 1

        def raw_count(n):
            return sum(len(IN_UNITS[k]) if k < U_OUT else 1 for k in range(n % 2, n + 1, 2))

        RAW_PL = [raw_count(UNITS - 2), raw_count(UNITS - 1)]

        block = ctx.enter_context(nc.Block())

        @block.sync
        def _(sp):
            sp.dma_start(ct[:], consts).then_inc(const_loaded, 16)
            sp.dma_start(posi[:], positions.to_broadcast([P, T])).then_inc(const_loaded, 16)
            sp.dma_start(trif[:], tri).then_inc(const_loaded, 16)
            for k in range(X_PIECES):
                cols = slice(k * D // X_PIECES, (k + 1) * D // X_PIECES)
                sp.dma_start(io[:, :, cols], x[0, :, cols].rearrange("(t p) d -> p t d", p=P)).then_inc(x_loaded[k], 16)

            def par(row, src):
                r = src.rearrange("(r p) -> r p", p=P)
                sp.dma_start(prow[row:row + r.shape[0], :], r).then_inc(par_loaded, 16)

            par(0, ln1_g[0])
            for l in range(DEPTH):
                b = PAR0 + PAR_L * l
                par(b + G_LN2, ln2_g[l])
                par(b + G_NEXT, ln1_g[l + 1] if l + 1 < DEPTH else final_g)
                par(b + G_QN, mla_q_norm[l])
                par(b + G_KVN, mla_kv_norm[l])
                par(b + G_PS, pool_scale[l])

            def load(n, l, pieces):
                plain_waits(sp, *split_counts(n - 2, l), *([(w_lo0, l + 1)] if n == 2 else []))
                col = 0
                for src, width in pieces:
                    sp.dma_start(raw[:, n % 2, :, col:col + width],
                                 src.rearrange("(k p) n -> p k n", p=P)).then_inc(raw_loaded[n % 2], 16)
                    col += width

            def load_in(n, l):
                load(n, l, [(w_in[l, :, a:a + w], w) for a, w in IN_UNITS[n]])

            def load_ff(l, c):
                for u in range(8):
                    plain_waits(sp, *split_counts(U_FF + u - 2, l, c))
                    if u < 4:
                        src = w_ff1[l, :, bass.ds(c * D + 256 * u, 256)]
                    else:
                        src = w_ff2[l, bass.ds(c * D, D), 256 * (u - 4):256 * (u - 3)]
                    sp.dma_start(raw[:, u % 2, :, :], src.rearrange("(k p) n -> p k n", p=P))\
                      .then_inc(raw_loaded[u % 2], 16)

            with sp.Fori(0, DEPTH) as l:
                load_in(0, l)
                load_in(1, l)
                sp.dma_start(graw[:], w_in[l, :, C_GATE:C_GATE + GATE_W].rearrange("(k p) n -> p k n", p=P))\
                  .then_inc(gate_loaded, 16)
                b = PS.bank("g7")
                plain_waits(sp, (full[b], l * PS.layer[b] + PS.pre[b]))
                for g in range(2):
                    sp.dma_start(prs[:, g * DH:(g + 1) * DH],
                                 nsa_cmp_pos[l].rearrange("v l d -> (v l) d")).then_inc(small_loaded, 16)
                    sp.dma_start(w1[:, g, :, :], nsa_cmp_w1[l, g].rearrange("(a b) d e -> (b d) a e", b=2))\
                      .then_inc(small_loaded, 16)
                    sp.dma_start(wq[:, g, :, 0:QK],
                                 mla_w_qup[l, g * P:(g + 1) * P, :].rearrange("p (h c) -> p h c", c=QK))\
                      .then_inc(small_loaded, 16)
                for k, g in enumerate((0, 0, 1)):
                    sp.dma_start(w2[:, k, :], nsa_cmp_w2[l, g]).then_inc(small_loaded, 16)
                for s in range(2):
                    sp.dma_start(wkv[:, s, :, :], mla_w_kvup[l].rearrange("p (h s c) -> p s h c", s=2, c=64)[:, s, :, :])\
                      .then_inc(small_loaded, 16)
                sp.wait_ge(zeros_set, 1)
                for g in range(4):
                    r = (g % 2) * POOL_G
                    sp.dma_start(pw[r:r + POOL_G, g // 2, r:r + POOL_G], pool_w[l, g]).then_inc(small_loaded, 16)
                for n in range(2, U_OUT):
                    load_in(n, l)
                for m in range(4):
                    load(U_OUT + m, l, [(w_out[l, :, 256 * m:256 * (m + 1)], 256)])
                with sp.Fori(0, CHUNKS) as c:
                    load_ff(l, c)
            for t in range(TT):
                sp.wait_ge(y_act, t + 1)
                sp.wait_ge(y_dve, t + 1)
                sp.dma_start(out[0, t * P:(t + 1) * P, :], io[:, t, :]).then_inc(stored, 16)
            sp.wait_ge(stored, 16 * TT)

        @block.tensor
        def _(pe):
            def begin(name, l=0, c=0):
                pe.wait_ge(moved[PS.bank(name)], PS.before(name, l, c))
                return psum[:, PS.bank(name), :]

            def done(mm, name):
                mm.then_inc(full[PS.bank(name)], 1)

            def three(o, wh, wl, h, lo, first, last):
                pe.matmul(o, wh, h, start=first, stop=False)
                pe.matmul(o, wl, h, start=False, stop=False)
                return pe.matmul(o, wh, lo, start=False, stop=last)

            def unit_split(n, l, c=0):
                for s, v in split_counts(n, l, c):
                    pe.wait_ge(s, v)

            def dense(name, slot, half, l, c=0, H=XH, L=XL, tiles=None, order=range(KT), first=True, last=True):
                o = begin(name, l, c) if first else psum[:, PS.bank(name), :]
                for n, k in enumerate(order):
                    if tiles is not None:
                        tiles(k)
                    cols = slice(half * P, (half + 1) * P)
                    mm = three(o, WH[:, slot, k, cols], WL[:, slot, k, cols], H[:, k, :], L[:, k, :],
                               first and n == 0, last and n == len(order) - 1)
                if last:
                    done(mm, name)

            def columns(name, l=0):
                o = begin(name, l)
                for t in range(TT):
                    mm = pe.matmul(o[:, t:t + 1], rs[:, t * P:(t + 1) * P], ones, start=True, stop=True)
                done(mm, name)

            def spread(name, k, l=0):
                o = begin(name, l)
                done(pe.matmul(o, ones.to_broadcast([P, P]), sqt[:, k, :], start=True, stop=True), name)

            pe.wait_ge(const_loaded, 48)
            pe.wait_ge(par_loaded, 16 * (1 + 5 * DEPTH))
            n = PAR0 + DEPTH * PAR_L
            done(pe.transpose(begin("par")[:, 0:n], prow[0:n, :], ct[0:n, K_ID:K_ID + n]), "par")
            for m in range(KT):
                pe.wait_ge(x_loaded[m * X_PIECES // KT], 16)
                o = begin(f"p{m}")
                for t in range(TT):
                    mm = pe.transpose(o[:, t * P:(t + 1) * P], io[:, t, m * P:(m + 1) * P], ident)
                done(mm, f"p{m}")

            def attention(l):
                def operands(u):
                    if u < 2 * NSA_H:
                        h, br = u // 2, u % 2
                        g = h // NSA_HPG
                        return QS[h], (KSH[:, br, g, :], KSL[br][:, g, :])
                    h = u - 2 * NSA_H
                    return QM[0:QK, h, :], (KM[0:QK, h, :],)

                def scores(u):
                    q, keys = operands(u)
                    if u == 0:
                        pe.wait_ge(kh_ready, l * 4 + 4)
                        pe.wait_ge(kl_ready, l * 8 + 8)
                    if u < 2 * NSA_H and u % 2 == 0:
                        pe.wait_ge(ql_ready, l * NSA_H + u // 2 + 1)
                    if u == 2 * NSA_H:
                        pe.wait_ge(qm_ready, l * MLA_H + MLA_H)
                        pe.wait_ge(kr_spread, l + 1)
                        for t in range(TT):
                            wait_moved(pe, f"vm{t}", l)
                    for i, b, col, _ in S_TILES:
                        name = f"s{u}{'abc'[b]}"
                        o = begin(name, l) if col == 0 else psum[:, b, :]
                        n = P * (i + 1)
                        for m, k in enumerate(keys):
                            pe.matmul(o[:, col:col + n], q[:, i * P:(i + 1) * P], k[:, 0:n], start=m == 0, stop=False)
                        mm = pe.matmul(o[:, col + n - P:col + n], identb[:], trib[:], start=False, stop=True)
                        if col or b != 1:
                            done(mm, name)

                def transposes(u):
                    pe.wait_ge(p_ready, l * 4 * N_UNITS_ATT + 4 * (u + 1))
                    for j, b, col, _ in T_TILES:
                        name = f"t{u}{'abc'[b]}"
                        o = begin(name, l) if col == 0 else psum[:, 3 + b, :]
                        for i in range(j, TT):
                            mm = pe.transpose(o[:, col + (i - j) * P:col + (i - j + 1) * P],
                                              pr[:, u % 2, S_COL[i] + j * P:S_COL[i] + (j + 1) * P], ident)
                        if col or b != 1:
                            done(mm, name)

                def values(u):
                    pair = PAIR_OF[u]
                    name = f"o{pair}"
                    if u == 0 or PAIR_OF[u - 1] != pair:
                        begin(name, l)
                    nsa = u < 2 * NSA_H
                    h = u // 2 if nsa else u - 2 * NSA_H
                    r = (h % 2) * 64
                    o = psum[r:r + 64, PS.bank(name), :]
                    first = (not nsa) or u % 2 == 0
                    for b in "abc":
                        wait_moved(pe, f"t{u}{b}", l)
                    if nsa and u % 2 == 0:
                        q, b = (h % 4) * NB, h // 4
                        pe.matmul(o, vcr[q:q + NB, b, :], PTc[q:q + NB, b, :], start=True, stop=False)
                        first = False
                    last = (not nsa) or u % 2 == 1
                    for j in range(TT):
                        n = T - j * P
                        if nsa:
                            g = (u % 2) * 2 + h // NSA_HPG
                            v = VN[:, j, g * DH:(g + 1) * DH]
                        else:
                            v = VM[:, j, h * VD:(h + 1) * VD]
                        mm = pe.matmul(o[:, j * P:T], v, PT[:, u % 2, T_COL[j]:T_COL[j] + n],
                                       start=first and j == 0, stop=last and j == TT - 1)
                    if u + 1 == N_UNITS_ATT or PAIR_OF[u + 1] != pair:
                        done(mm, name)

                for s in range(N_UNITS_ATT + 2):
                    if s < N_UNITS_ATT:
                        scores(s)
                    if s == 0:
                        pe.wait_ge(cp_ready, l + 1)
                        pe.wait_ge(kr_spread, l + 1)
                        for b, n in ((0, 4), (1, 2)):
                            plain_waits(pe, free_before(f"ct{b}", l))
                            o = psum[:, PS.bank(f"ct{b}"), :]
                            for t in range(TT):
                                mm = pe.transpose(o[0:n * NB, t * P:(t + 1) * P],
                                                  sc[:, t, 4 * b:4 * b + n, :].rearrange("p h n -> p (h n)"), ident)
                            done(mm, f"ct{b}")
                    if s == N_UNITS_ATT:
                        unit_split(U_OUT, l)
                        dense("x0", 0, 0, l, 0, BH, BL, lambda k: mixed(k, l), B_ORDER[:6], last=False)
                    if 1 <= s <= N_UNITS_ATT:
                        transposes(s - 1)
                    if s >= 2:
                        values(s - 2)

            def hidden(k, l, c):
                pe.wait_ge(bh_ready, l * B_PL + c * KT + (KT + k + 1))
                pe.wait_ge(bl_ready, l * (KT * CHUNKS) + c * KT + (k + 1))

            def mixed(k, l):
                pe.wait_ge(bh_ready, l * B_PL + B_ORDER.index(k) + 1)
                wait_moved(pe, f"o{k}" if k < 6 else f"py{k - 6}", l)

            def gained(k, l):
                pe.wait_ge(xh_ready, l * 2 * KT + (k + 1))
                pe.wait_ge(xl_ready, l * 2 * KT + (k + 1))

            def ff_chunk(l, c):
                for m in range(2, KT):
                    if m % 2 == 0:
                        unit_split(U_FF + m // 2, l, c)
                    dense(f"f{m}", (m // 2) % 2, m % 2, l, c)
                for m in range(KT):
                    if m % 2 == 0:
                        unit_split(U_FF + 4 + m // 2, l, c)
                    dense(f"g{m}", (m // 2) % 2, m % 2, l, c, BH, BL,
                          (lambda k: hidden(k, l, c)) if m == 0 else None)

            with pe.Fori(0, DEPTH) as l:
                pe.wait_ge(w_lo0, l + 1)
                dense("cq0", 0, 0, l, tiles=lambda k: gained(k, l))
                unit_split(0, l)
                dense("cq1", 0, 1, l)
                pe.wait_ge(sq_added, (l * 2 + 1) * KT)
                columns("ncol", l)
                plain_waits(pe, (small_loaded, (l + 1) * (16 * NSMALL)), free_before("post", l))
                done(pe.transpose(psum[:, PS.bank("post"), 0:2 * CMP_LEN], prs[:, :], ct[0:2 * CMP_LEN, K_ID:K_ID + 2 * CMP_LEN]),
                     "post")
                unit_split(1, l)
                dense("ckv", 1, 0, l)
                pe.wait_ge(diag_ready, l * 2 + 1)
                spread("nbc", 0, l)
                dense("kr", 1, 1, l)
                unit_split(2, l)
                dense("kc", 0, 0, l)
                dense("vc", 0, 1, l)
                pe.wait_ge(msq_ready, l * 3 + 3)
                o = begin("mcol", l)
                for t in range(TT):
                    cols = slice(t * P, (t + 1) * P)
                    pe.matmul(o[:, t:t + 1], sqt[:, 0, cols], ones, start=True, stop=False)
                    pe.matmul(o[:, t:t + 1], sqt[:, 1, cols], ones, start=False, stop=True)
                for t in range(TT):
                    mm = pe.matmul(o[:, TT + t:TT + t + 1], sqt[:, 2, t * P:(t + 1) * P], ones, start=True, stop=True)
                done(mm, "mcol")
                unit_split(3, l)
                dense("ks", 1, 0, l)
                dense("kw", 1, 1, l)
                pe.wait_ge(mdiag_ready, l + 1)
                spread("mbq", 1, l)
                spread("mbk", 2, l)
                unit_split(4, l)
                for t in range(TT):
                    o = begin(f"v{t}", l)
                    cols = slice(t * P, (t + 1) * P)
                    for ww, wl_, n0, n1 in ((WH[:, 0], WL[:, 0], 0, 256), (GH, GL, 256, 256 + GATE_W)):
                        for k in range(KT):
                            pe.matmul(o[:, n0:n1], XH[:, k, cols], ww[:, k, :], start=(k == 0), stop=False)
                            pe.matmul(o[:, n0:n1], XH[:, k, cols], wl_[:, k, :], start=False, stop=False)
                            mm = pe.matmul(o[:, n0:n1], XL[:, k, cols], ww[:, k, :], start=False, stop=(k == KT - 1))
                    done(mm, f"v{t}")
                unit_split(5, l)
                dense("q0", 1, 0, l)
                dense("q1", 1, 1, l)
                pe.wait_ge(bcmp_ready, l * 8 + 8)
                for v, name in enumerate(("hk", "hv")):
                    o = begin(name, l)
                    for a in range(16):
                        mm = pe.matmul(o[0:DH, 0:2 * NB], w1[:, v, a, :], bcmp[:, v, a, :], start=(a == 0), stop=(a == 15))
                    done(mm, name)
                unit_split(6, l)
                dense("q2", 0, 0, l)
                unit_split(7, l)
                dense("u0", 1, 0, l)
                dense("u1", 1, 1, l)

                def up_q(h):
                    o = begin(f"uq{h}", l)
                    for k in range(2):
                        mm = pe.matmul(o, wq[:, k, h, :], cq[:, k, :], start=(k == 0), stop=(k == 1))
                    done(mm, f"uq{h}")

                pe.wait_ge(wq_cols, l + 1)
                wait_moved(pe, "mbq", l)
                up_q(0)
                up_q(1)
                pe.wait_ge(hg_ready, l + 1)
                done(pe.matmul(begin("k2", l)[:, 0:2 * NB], w2[:, 0:2, :].rearrange("p a f -> p (a f)"), hg[:, 0, :],
                               start=True, stop=True), "k2")
                plain_waits(pe, free_before("w2", l))
                for h in range(NSA_H):
                    q, b, g = (h % 4) * NB, h // 4, h // NSA_HPG
                    mm = pe.matmul(psum[q:q + NB, PS.bank("w2"), b * DH:(b + 1) * DH], hg[:, 1, g * NB:(g + 1) * NB],
                                   w2[:, 2, :], start=True, stop=True)
                done(mm, "w2")
                up_q(2)
                up_q(3)
                pe.wait_ge(pooled_ready, l * 2 + 2)
                for k in range(2):
                    done(pe.matmul(begin(f"py{k}", l), pw[:, k, :], pb[:, k, CMP_STRIDE:], start=True, stop=True), f"py{k}")
                wait_moved(pe, "k2", l)
                wait_moved(pe, "q2", l)
                for b in range(2):
                    o = begin(f"cs{b}", l)
                    for t in range(TT):
                        for h in range(b, NSA_H, 2):
                            r, g = (h % 2) * DH, h // NSA_HPG
                            col = (t * 3 + h // 2) * NB
                            mm = pe.matmul(o[:, col:col + NB], qT[r:r + DH, h // 2, t * P:(t + 1) * P],
                                           kc2[r:r + DH, g * NB:(g + 1) * NB], start=True, stop=True)
                    done(mm, f"cs{b}")
                up_q(4)
                up_q(5)
                wait_moved(pe, "mbk", l)
                for p in range(3):
                    done(pe.matmul(begin(f"kn{p}", l), wkv[:, 0, 2 * p:2 * p + 2, :].rearrange("p h c -> p (h c)"), ckv[:], start=True, stop=True), f"kn{p}")
                for t in range(TT):
                    done(pe.matmul(begin(f"vm{t}", l)[:, 0:MLA_H * VD], ckv[:, t * P:(t + 1) * P], wkv[:, 1, :, :].rearrange("p h c -> p (h c)"),
                                   start=True, stop=True), f"vm{t}")
                attention(l)
                dense("x0", 0, 0, l, 0, BH, BL, lambda k: mixed(k, l), B_ORDER[6:], first=False)
                for m in range(1, KT):
                    if m % 2 == 0:
                        unit_split(U_OUT + m // 2, l)
                    dense(f"x{m}", (m // 2) % 2, m % 2, l, 0, BH, BL)
                unit_split(U_FF, l)
                dense("f0", 0, 0, l, tiles=lambda k: gained(KT + k, l))
                pe.wait_ge(sq_added, (l * 2 + 2) * KT)
                columns("ncol2", l)
                dense("f1", 0, 1, l)
                pe.wait_ge(diag_ready, l * 2 + 2)
                spread("nbc2", 0, l)
                with pe.Fori(0, CHUNKS - 1) as c:
                    ff_chunk(l, c)
                    unit_split(U_FF, l, c + 1)
                    dense("f0", 0, 0, l, c + 1)
                    dense("f1", 0, 1, l, c + 1)
                ff_chunk(l, CHUNKS - 1)

            pe.wait_ge(sq_added, (2 * DEPTH + 1) * KT)
            columns("ncol3")
            pe.wait_ge(identr_ready, 1)
            pe.wait_ge(xl_ready, (2 * DEPTH + 1) * KT)
            for n in range(2 * TT):
                t, half = n // 2, n % 2
                o = begin(f"y{n}")
                for m in range(4):
                    k = half * 4 + m
                    cols = slice(m * P, (m + 1) * P)
                    pe.matmul(o[:, cols], XH[:, k, t * P:(t + 1) * P], identr[:], start=True, stop=False)
                    mm = pe.matmul(o[:, cols], XL[:, k, t * P:(t + 1) * P], identr[:], start=False, stop=True)
                done(mm, f"y{n}")

        @block.scalar
        def _(act):
            def copy(o, i, **kw):
                return act.activation(o, i, ACT.Copy, **kw)

            def split_hi(n, l, job, c=None):
                s = n % 2
                if c is None:
                    act.wait_ge(raw_loaded[s], l * (16 * RAW_PL[s]) + 16 * raw_count(n))
                else:
                    act.wait_ge(raw_loaded[s], l * (16 * RAW_PL[s]) + c * 64 + 16 * raw_count(n))
                if job is not None:
                    wait_full(act, *job)
                w = IN_WIDTH[n] if n < U_OUT else 256
                if n == 1:
                    act.wait_ge(gate_loaded, (l + 1) * 16)
                    copy(GH[:], graw[:])
                    act.wait_ge(kr_cols, l * 3 + 3)
                for a in ((0, P) if n == 0 else (0,)):
                    b = P if n == 0 and a == 0 else w
                    copy(WH[:, s, :, a:b], raw[:, s, :, a:b]).then_inc(w_hi, 1)

            def prep(m, norm, gain):
                copy(XH[:, m, :], xT[:, m, :], scale=gain).then_inc(xh_ready, 1)
                if m >= 2:
                    act.wait_ge(sq_added, norm * KT + (m - 1))
                act.activation(sqt[:, m % 2, :], xT[:, m, :], ACT.Square).then_inc(sq_ready, 1)

            act.wait_ge(trig_arg, 1)
            act.activation(sintab[:], trig[:, 1, :], ACT.Sin).then_inc(sin_ready, 1)
            act.wait_ge(trig_arg, 2)
            act.activation(costab[:], trig[:, 2, :], ACT.Sin).then_inc(sin_ready, 1)
            wait_moved(act, "par")
            act.wait_ge(masks_set, 2)
            for m in range(KT):
                wait_moved(act, f"p{m}")
                prep(m, 0, params[:, m:m + 1])

            def ff_chunk(l, c, last):
                for m in range(KT):
                    wait_moved(act, f"f{m}", l, c)
                    act.activation(BH[:, m, :], relu[:, m % 2, :], ACT.Square).then_inc(bh_ready, 1)
                    if m % 2:
                        split_hi(U_FF + m // 2 + 2, l, (f"f{m}", l, c), c)
                for m in range(KT):
                    if last:
                        wait_moved(act, f"g{m}", l, c)
                        prep(m, l * 2 + 2, gl[:, G_NEXT + m:G_NEXT + m + 1])
                    if m % 2 and not (last and m // 2 >= 2):
                        split_hi(U_FF + 4 + m // 2 + 2, l, (f"g{m}", l, c), c)

            with act.Fori(0, DEPTH) as l:
                def queries_high(h):
                    rows = slice((h % 2) * DH, (h % 2) * DH + DH)
                    wait_moved(act, f"q{h // 2}", l)
                    copy(QS[h][rows, :], qT[rows, h // 2, :]).then_inc(qh_ready, 1)

                split_hi(0, l, None)
                split_hi(1, l, None)
                split_hi(2, l, ("cq1", l))
                wait_full(act, "nbc", l)
                release(copy(rs[:], psum[:, PS.bank("nbc"), :]), "nbc")
                split_hi(3, l, ("kr", l))
                for k, (src, name) in enumerate(((cq[:, 0, :], "cq0"), (cq[:, 1, :], "cq1"), (ckv[:], "ckv"))):
                    wait_moved(act, name, l)
                    act.activation(sqt[:, k, :], src, ACT.Square).then_inc(msq_ready, 1)
                split_hi(4, l, ("vc", l))
                split_hi(5, l, ("kw", l))
                wait_moved(act, "ks", l)
                wait_moved(act, "kw", l)
                for g, half in ((0, 0), (1, 1), (0, 1), (1, 0)):
                    copy(KSH[half * DH:(half + 1) * DH, :, g, :], kraw[g * DH:(g + 1) * DH, :, :])\
                        .then_inc(kh_ready, 1)
                for t in range(TT):
                    wait_full(act, f"v{t}", l)
                    copy(VN[:, t, :], psum[:, PS.bank(f"v{t}"), 0:256], scale=rcol[:, t:t + 1])
                    release(copy(gz[:, t, :], psum[:, PS.bank(f"v{t}"), 256:256 + GATE_W], scale=rcol[:, t:t + 1]),
                            f"v{t}")
                split_hi(6, l, ("v3", l))
                wait_moved(act, "v3", l)
                act.activation(gates[:], gz[:], ACT.Exp, scale=-1.0).then_inc(gexp_ready, 1)
                split_hi(7, l, ("q1", l))
                act.wait_ge(gelu_arg, l + 1)
                act.activation(hg[:], hg[:], ACT.Exp, scale=-2.0 * float(np.sqrt(2.0 / np.pi)))\
                   .then_inc(gelu_exp, 1)
                wait_full(act, "hv", l)
                for h in range(4):
                    queries_high(h)
                split_hi(8, l, ("q2", l))
                split_hi(9, l, ("u1", l))

                def up_q(h):
                    wait_full(act, f"uq{h}", l)
                    release(copy(QM[:, h, :], psum[:, PS.bank(f"uq{h}"), :]), f"uq{h}")

                for h in range(4):
                    up_q(h)
                for k in range(2):
                    wait_full(act, f"py{k}", l)
                    copy(BH[:, 6 + k, :], psum[:, PS.bank(f"py{k}"), :], scale=gl[:, G_PS + k:G_PS + k + 1])\
                        .then_inc(bh_ready, 1)
                for h in range(4, MLA_H):
                    up_q(h)
                act.wait_ge(csub_ready, l + 1)
                act.activation(sc[:], sc[:], ACT.Exp).then_inc(cexp_ready, 1)
                for p in range(3):
                    wait_full(act, f"kn{p}", l)
                    copy(KM[0:NOPE, 2 * p, :], psum[0:NOPE, PS.bank(f"kn{p}"), :])
                    release(copy(KM[0:NOPE, 2 * p + 1, :], psum[NOPE:P, PS.bank(f"kn{p}"), :]), f"kn{p}")

                for s in range(N_UNITS_ATT + 3):
                    if s == 2:
                        wait_full(act, "vm3", l)
                        queries_high(4)
                        queries_high(5)
                    if s == 1:
                        wait_full(act, "ct0", l)
                        release(copy(PTc[:, 0, :], psum[:, PS.bank("ct0"), :]), "ct0")
                    if 1 <= s <= N_UNITS_ATT:
                        u = s - 1
                        wait_full(act, f"t{u}a", l)
                        release(copy(PT[:, u % 2, 0:512], psum[:, 3, :]), f"t{u}a")
                        wait_full(act, f"t{u}c", l)
                        release(copy(PT[:, u % 2, 1024:PW], psum[:, 5, 0:256]), f"t{u}c")
                    if s < N_UNITS_ATT:
                        scale = 1.0 if s < 2 * NSA_H else QK ** -0.5
                        for n, (i, b, col, pc) in enumerate(S_TILES):
                            if n < 2:
                                act.wait_ge(max_ready, l * 2 * N_UNITS_ATT + 2 * s + n + 1)
                            n = P * (i + 1)
                            e = act.activation(pr[:, s % 2, pc:pc + n], psum[:, b, col:col + n], ACT.Exp,
                                               bias=nms[:, s % 2, i:i + 1], scale=scale,
                                               accum_out=ssum[:, s % 2, i:i + 1])
                            if col or b != 1:
                                release(e, f"s{s}{'abc'[b]}")
                    u = s - 3
                    if u >= 0 and (u + 1 == N_UNITS_ATT or PAIR_OF[u + 1] != PAIR_OF[u]):
                        pair = PAIR_OF[u]
                        wait_full(act, f"o{pair}", l)
                        copy(BH[:, pair, :], psum[:, PS.bank(f"o{pair}"), :]).then_inc(bh_ready, 1)
                for m in range(KT):
                    wait_moved(act, f"x{m}", l)
                    prep(m, l * 2 + 1, gl[:, G_LN2 + m:G_LN2 + m + 1])
                    if m % 2:
                        split_hi(U_OUT + m // 2 + 2, l, (f"x{m}", l))
                wait_full(act, "nbc2", l)
                release(copy(rs[:], psum[:, PS.bank("nbc2"), :]), "nbc2")
                with act.Fori(0, CHUNKS - 1) as c:
                    ff_chunk(l, c, False)
                ff_chunk(l, CHUNKS - 1, True)

            copy(identr[:], ident).then_inc(identr_ready, 1)
            act.wait_ge(rcol_ready, 2 * DEPTH + 1)
            for t in range(TT):
                n = 2 * t
                wait_full(act, f"y{n}")
                copy(io[:, t, 0:512], psum[:, PS.bank(f"y{n}"), :], scale=rcol[:, t:t + 1]).then_inc(y_act, 1)

        @block.gpsimd
        def _(pool):
            chain = Chain(pool, pool_step, POOL_PL)

            def copy(o, i, r=slice(0, P)):
                one = ct[r, K_ONE:K_ONE + 1]
                for _ in i.shape[2:]:
                    one = one.unsqueeze(1)
                return pool.tensor_tensor(o, i, one.to_broadcast(list(i.shape)), ALU.mult)

            pool.memset(pw[:], 0.0).then_inc(zeros_set, 1)
            pool.memset(kcv[:, :, T:], 0.0).then_inc(w_hi, 1)
            pool.memset(up[:, :, 0:CMP_STRIDE], 0.0).then_inc(w_lo, 1)
            pool.wait_ge(const_loaded, 48)
            pool.tensor_copy(identb[:], ident).then_inc(masks_set, 1)
            pool.tensor_copy(trib[:], trif[:]).then_inc(masks_set, 1)

            def split_lo(n, l, c=None):
                pool.wait_ge(*split_counts(n, l, 0 if c is None else c)[0])
                w = IN_WIDTH[n] if n < U_OUT else 256
                s, a = n % 2, P if n == 0 else 0
                pool.tensor_tensor(WL[:, s, :, a:w], raw[:, s, :, a:w], f32(WH[:, s, :, a:w]), ALU.subtract)\
                    .then_inc(w_lo, 1)

            def add_square(m, norm):
                pool.wait_ge(sq_ready, norm * KT + (m + 1))
                if m == 0:
                    copy(rs[:], sqt[:, 0, :]).then_inc(sq_added, 1)
                else:
                    pool.wait_ge(sq_added, norm * KT + m)
                    pool.tensor_tensor(rs[:], rs[:], sqt[:, m % 2, :], ALU.add).then_inc(sq_added, 1)

            for m in range(KT):
                add_square(m, 0)

            def ff_chunk(l, c, last):
                for m in range(KT):
                    wait_moved(pool, f"f{m}", l, c)
                    pool.tensor_tensor(asq[:, m % 2, :], relu[:, m % 2, :], relu[:, m % 2, :], ALU.mult)\
                        .then_inc(asq_ready, 1)
                    if m % 2:
                        split_lo(U_FF + m // 2 + 2, l, c)
                for m in range(KT):
                    if last:
                        add_square(m, l * 2 + 2)
                    if m % 2 and not (last and m // 2 >= 2):
                        split_lo(U_FF + 4 + m // 2 + 2, l, c)

            with pool.Fori(0, DEPTH) as l:
                chain.layer(l)
                split_lo(0, l)
                pool.wait_ge(raw_loaded[1], l * (16 * RAW_PL[1]) + 16)
                kr = raw[:, 1, :, 128:256]
                copy(kr[:, :, 32:48], kr[:, :, 16:32]).then_inc(kr_cols, 1)
                copy(kr[:, :, 48:64], kr[:, :, 0:16]).then_inc(kr_cols, 1)
                pool.wait_ge(kr_cols, l * 3 + 2)
                copy(kr[:, :, 64:128], kr[:, :, 0:64]).then_inc(kr_cols, 1)
                pool.wait_ge(*split_counts(1, l)[0])
                pool.tensor_tensor(GL[:], graw[:], f32(GH[:]), ALU.subtract)
                split_lo(1, l)
                pool.wait_ge(small_loaded, (l + 1) * (16 * NSMALL))
                for g in range(2):
                    copy(wq[:, g, :, QK:QK + 16], wq[:, g, :, QK - 16:QK])
                    copy(wq[:, g, :, QK + 16:P], wq[:, g, :, NOPE:NOPE + 16]).then_inc(wq_cols, 1)
                split_lo(2, l)
                split_lo(3, l)
                pool.wait_ge(krot_ready, l + 1)
                pool.wait_ge(*split_counts(3, l)[1])
                chain.link(pool.tensor_tensor(krt[64:96, :], krt[64:96, :], krz[64:96, :], ALU.add))
                for n in range(4, 9):
                    split_lo(n, l)
                E = T + CMP_STRIDE
                for k in range(2):
                    wait_moved(pool, f"u{k}", l)
                    chain.link(pool.tensor_tensor(pa[:, k, 2:E], up[:, k, 2:E], up[:, k, 1:E - 1], ALU.add))
                    last = pool.tensor_tensor(pb[:, k, 4:E], pa[:, k, 4:E], pa[:, k, 2:E - 2], ALU.add)
                    if k:
                        chain.link(last)
                        chain.link(pool.tensor_tensor(pa[:, k, 8:E], pb[:, k, 8:E], pb[:, k, 4:E - 4], ALU.add))
                        last = pool.tensor_tensor(pb[64:P, k, 16:E], pa[64:P, k, 16:E], pa[64:P, k, 8:E - 8], ALU.add)
                    last.then_inc(pool_add, 1)
                pool.wait_ge(pool_add, l * 2 + 2)
                split_lo(9, l)
                pool.wait_ge(*split_counts(9, l)[1])
                copy(KM[64:96, :, :], krt[64:96, :].unsqueeze(1).to_broadcast([32, MLA_H, T]), slice(64, 96))\
                    .then_inc(kr_spread, 1)
                pool.wait_ge(kr_spread, l + 1)
                for h in range(MLA_H):
                    pool.wait_ge(qrot_ready, l * MLA_H + h + 1)
                    a, b = rot(h)
                    pool.tensor_tensor(QM[64:96, h, :], a, b, ALU.add).then_inc(qm_ready, 1)
                    pool.wait_ge(qm_ready, l * MLA_H + h + 1)
                for u in range(N_UNITS_ATT):
                    for k, (i, _, _, pc) in enumerate(S_TILES):
                        if k < 2:
                            pool.wait_ge(fac_ready, l * 2 * N_UNITS_ATT + 2 * u + k + 1)
                        n = P * (i + 1)
                        p = pr[:, u % 2, pc:pc + n]
                        pool.tensor_tensor(p, p, fac[:, u % 2, i:i + 1].to_broadcast([P, n]), ALU.mult)\
                            .then_inc(p_ready, 1)
                for m in range(KT):
                    add_square(m, l * 2 + 1)
                    if m % 2:
                        split_lo(U_OUT + m // 2 + 2, l)
                with pool.Fori(0, CHUNKS - 1) as c:
                    ff_chunk(l, c, False)
                ff_chunk(l, CHUNKS - 1, True)
                assert chain.n == POOL_PL, chain.n

        @block.vector
        def _(dve):
            chain = Chain(dve, dve_step, DVE_PL, DVE_PRE)

            def bank(name):
                return psum[:, PS.bank(name), :]

            def low(m, gain, need):
                dve.wait_ge(xh_ready, need)
                dve.scalar_tensor_tensor(out=XL[:, m, :], in0=xT[:, m, :], scalar=gain, in1=f32(XH[:, m, :]),
                                         op0=ALU.mult, op1=ALU.subtract).then_inc(xl_ready, 1)

            def rsqrt(n, o, ready):
                a, t, y = na[:, 0:n], nt[:, 0:n], ni[:, 0:n]
                chain.link(dve.tensor_scalar(y, a.bitcast(I32), 1, None, ALU.logical_shift_right))
                chain.link(dve.tensor_scalar(y, y, -1.0, float(0x5f3759df), ALU.mult, ALU.add))
                y = y.bitcast(F32)
                for k in range(3):
                    chain.link(dve.tensor_tensor(t, y, y, ALU.mult))
                    chain.link(dve.tensor_tensor(t, t, a, ALU.mult))
                    chain.link(dve.tensor_scalar(t, t, -0.5, 1.5, ALU.mult, ALU.add))
                    if k < 2:
                        chain.link(dve.tensor_tensor(y, y, t, ALU.mult))
                dve.tensor_tensor(o, y, t, ALU.mult).then_inc(*ready)

            def residual_norm(name, norm, spread, l=0):
                wait_full(dve, name, l)
                release(dve.tensor_scalar(na[:, 0:TT], bank(name)[:, 0:TT], 1.0 / D, EPS, ALU.mult, ALU.add), name)
                wait_moved(dve, name, l)
                rsqrt(TT, rcol[:, 0:TT], (rcol_ready, 1))
                dve.wait_ge(rcol_ready, norm + 1)
                if spread:
                    for t in range(TT):
                        d = dve.tensor_scalar(sqt[:, 0, t * P:(t + 1) * P], ident, rcol[:, t:t + 1], None, ALU.mult)
                    d.then_inc(diag_ready, 1)

            dve.wait_ge(const_loaded, 48)
            ang, r0, r1 = trig[:, 0, :], trig[:, 1, :], trig[:, 2, :]
            chain.base, two_pi = 0, 2.0 * np.pi
            c1 = 6.28125
            c2 = float(np.float32(two_pi - c1).view(np.uint32) & np.uint32(0xfffff000))
            c2 = float(np.uint32(c2).view(np.float32))
            c3 = float(np.float32(two_pi - c1 - c2))
            chain.link(dve.tensor_copy(ang, posi[:]))
            chain.link(dve.tensor_scalar(ang, ang, ct[:, K_INVF:K_INVF + 1], None, ALU.mult))
            turns = qT[:, 0, :]
            for r, quarter in ((r0, 0.0), (r1, 0.25)):
                chain.link(dve.tensor_scalar(turns, ang, float(1.0 / two_pi), quarter, ALU.mult, ALU.add))
                chain.link(dve.tensor_scalar(turns, turns, 12582912.0, None, ALU.add))
                chain.link(dve.tensor_scalar(turns, turns, -12582912.0, None, ALU.add))
                chain.link(dve.scalar_tensor_tensor(out=r, in0=turns, scalar=-c1, in1=ang, op0=ALU.mult, op1=ALU.add))
                chain.link(dve.scalar_tensor_tensor(out=r, in0=turns, scalar=-c2, in1=r, op0=ALU.mult, op1=ALU.add))
                chain.link(dve.scalar_tensor_tensor(out=r, in0=turns, scalar=-c3, in1=r, op0=ALU.mult, op1=ALU.add))
                chain.link(dve.tensor_scalar(r, r, float(2.0 * np.pi * quarter), 3.1415925, ALU.add, ALU.min))
                chain.link(dve.tensor_scalar(r, r, -3.1415925, None, ALU.max))
                dve.tensor_scalar(r, r, 1.0, None, ALU.mult).then_inc(trig_arg, 1)
            wait_full(dve, "par")
            n = PAR0 + DEPTH * PAR_L
            release(dve.tensor_copy(params[:], bank("par")[:, 0:n]), "par")
            for m in range(KT):
                wait_full(dve, f"p{m}")
                release(dve.tensor_copy(xT[:, m, :], bank(f"p{m}")), f"p{m}")
                wait_moved(dve, f"p{m}")
                low(m, params[:, m:m + 1], m + 1)
            dve.wait_ge(sin_ready, 2)
            chain.link(dve.tensor_scalar(sintab[:], sintab[:], ct[:, K_SIGN:K_SIGN + 1], None, ALU.mult))
            assert chain.n == DVE_PRE, chain.n
            chain.base = DVE_PRE
            dve.wait_ge(w_hi, 1)
            dve.wait_ge(w_lo, 1)

            def ff_chunk(l, c, last):
                for m in range(KT):
                    wait_full(dve, f"f{m}", l, c)
                    release(dve.scalar_tensor_tensor(out=relu[:, m % 2, :], in0=bank(f"f{m}"), scalar=0.0, in1=rs[:],
                                                     op0=ALU.max, op1=ALU.mult), f"f{m}")
                    dve.wait_ge(bh_ready, l * B_PL + c * KT + (KT + m + 1))
                    dve.wait_ge(asq_ready, l * (KT * CHUNKS) + c * KT + (m + 1))
                    dve.tensor_tensor(BL[:, m, :], asq[:, m % 2, :], f32(BH[:, m, :]), ALU.subtract)\
                       .then_inc(bl_ready, 1)
                for m in range(KT):
                    wait_full(dve, f"g{m}", l, c)
                    release(dve.tensor_tensor(xT[:, m, :], bank(f"g{m}"), xT[:, m, :], ALU.add), f"g{m}")
                    if last:
                        low(m, gl[:, G_NEXT + m:G_NEXT + m + 1], l * 2 * KT + (2 * KT + m + 1))

            with dve.Fori(0, DEPTH) as l:
                chain.layer(l)
                dve.wait_ge(w_hi, l * HI_PL + 2)
                dve.tensor_tensor(WL[:, 0, :, 0:P], raw[:, 0, :, 0:P], f32(WH[:, 0, :, 0:P]), ALU.subtract)\
                    .then_inc(w_lo0, 1)
                plain_waits(dve, (xl_ready, (l * 2 + 1) * KT))
                dve.tensor_copy(gl[:], params[:, bass.ds(l * PAR_L + PAR0, PAR_L)]).then_inc(gl_ready, 1)
                dve.wait_ge(gl_ready, l + 1)
                residual_norm("ncol", l * 2, True, l)
                wait_full(dve, "post", l)
                release(dve.tensor_copy(pos2[:], bank("post")[:, 0:2 * CMP_LEN]), "post")
                wait_moved(dve, "nbc", l)

                def scaled(name, o):
                    wait_full(dve, name, l)
                    release(dve.tensor_tensor(o, bank(name), rs[:], ALU.mult), name)

                def queries(k):
                    name = f"q{k}"
                    wait_full(dve, name, l)
                    release(dve.scalar_tensor_tensor(out=qT[:, k, :], in0=bank(name), scalar=DH ** -0.5, in1=rs[:],
                                                     op0=ALU.mult, op1=ALU.mult), name)

                def queries_low(h):
                    r = (h % 2) * DH
                    dve.wait_ge(qh_ready, l * NSA_H + h + 1)
                    dve.tensor_tensor(QS[h][DH - r:2 * DH - r, :], qT[r:r + DH, h // 2, :], f32(QS[h][r:r + DH, :]),
                                      ALU.subtract).then_inc(ql_ready, 1)

                scaled("cq0", cq[:, 0, :])
                scaled("cq1", cq[:, 1, :])
                scaled("ckv", ckv[:])
                scaled("kr", krz[:])
                wait_moved(dve, "kr", l)
                chain.link(dve.tensor_tensor(krt[64:96, :], krz[64:96, :], costab[64:96, :], ALU.mult))
                dve.tensor_tensor(krz[64:96, :], krz[96:128, :], sintab[96:128, :], ALU.mult).then_inc(krot_ready, 1)
                scaled("kc", kcv[:, 0, 0:T])
                scaled("vc", kcv[:, 1, 0:T])
                wait_full(dve, "mcol", l)
                chain.link(dve.tensor_scalar(na[:, 0:TT], bank("mcol")[:, 0:TT], 1.0 / Q_LORA, EPS, ALU.mult, ALU.add))
                release(dve.tensor_scalar(na[:, TT:2 * TT], bank("mcol")[:, TT:2 * TT], 1.0 / KV_LORA, EPS,
                                          ALU.mult, ALU.add), "mcol")
                wait_moved(dve, "mcol", l)
                rsqrt(2 * TT, rcol[:, TT:3 * TT], (dve_step, 1))
                chain.n += 1
                dve.wait_ge(dve_step, l * DVE_PL + (DVE_PRE + chain.n))
                for t in range(2 * TT):
                    d = dve.tensor_scalar(sqt[:, 1 + t // TT, (t % TT) * P:(t % TT + 1) * P], ident,
                                          rcol[:, TT + t:TT + t + 1], None, ALU.mult)
                d.then_inc(mdiag_ready, 1)
                scaled("ks", kraw[:, 0, :])
                scaled("kw", kraw[:, 1, :])
                wait_full(dve, "mbq", l)
                for k in range(2):
                    d = dve.scalar_tensor_tensor(out=cq[:, k, :], in0=cq[:, k, :], scalar=gl[:, G_QN + k:G_QN + k + 1],
                                                 in1=bank("mbq"), op0=ALU.mult, op1=ALU.mult)
                release(d, "mbq")
                wait_full(dve, "mbk", l)
                release(dve.scalar_tensor_tensor(out=ckv[:], in0=ckv[:], scalar=gl[:, G_KVN:G_KVN + 1],
                                                 in1=bank("mbk"), op0=ALU.mult, op1=ALU.mult), "mbk")
                wait_moved(dve, "post", l)
                wait_moved(dve, "vc", l)
                for v in range(2):
                    for par in range(2):
                        for g in range(2):
                            src = kcv[g * DH:(g + 1) * DH, v, :]
                            rows = src.ap[0]
                            win = bass.AP(tensor=src.tensor, offset=src.offset + par,
                                          ap=[rows, [2, 16], [CMP_STRIDE, NB]])
                            pos = pos2[g * DH:(g + 1) * DH, v * CMP_LEN + par:(v + 1) * CMP_LEN:2]
                            dve.tensor_tensor(bcmp[par * DH:(par + 1) * DH, v, :, g * NB:(g + 1) * NB], win,
                                              pos.unsqueeze(2).to_broadcast([DH, 16, NB]), ALU.add)\
                               .then_inc(bcmp_ready, 1)
                dve.wait_ge(gexp_ready, l + 1)
                chain.link(dve.tensor_scalar(gates[:], gates[:], 1.0, None, ALU.add))
                dve.reciprocal(gates[:], gates[:]).then_inc(gates_ready, 1)
                queries(0)
                queries(1)
                wait_full(dve, "hk", l)
                release(dve.tensor_copy(hx[:, 0, :], bank("hk")[0:DH, 0:2 * NB]), "hk")
                wait_full(dve, "hv", l)
                release(dve.tensor_copy(hx[:, 1, :], bank("hv")[0:DH, 0:2 * NB]), "hv")
                wait_moved(dve, "hk", l)
                wait_moved(dve, "hv", l)
                chain.link(dve.tensor_tensor(hg[:], hx[:], hx[:], ALU.mult))
                chain.link(dve.tensor_scalar(hg[:], hg[:], 0.044715, 1.0, ALU.mult, ALU.add))
                dve.tensor_tensor(hg[:], hg[:], hx[:], ALU.mult).then_inc(gelu_arg, 1)
                queries(2)
                dve.wait_ge(gelu_exp, l + 1)
                chain.link(dve.tensor_scalar(hg[:], hg[:], 1.0, None, ALU.add))
                chain.link(dve.reciprocal(hg[:], hg[:]))
                dve.tensor_tensor(hg[:], hg[:], hx[:], ALU.mult).then_inc(hg_ready, 1)
                for h in range(4):
                    queries_low(h)
                scaled("u0", up[:, 0, CMP_STRIDE:])
                scaled("u1", up[:, 1, CMP_STRIDE:])
                dve.wait_ge(kh_ready, l * 4 + 2)
                for g in range(2):
                    rows = slice(g * DH, (g + 1) * DH)
                    for br in range(2):
                        dve.tensor_tensor(KSL[br][rows, g, :], kraw[rows, br, :], f32(KSH[rows, br, g, :]), ALU.subtract)\
                           .then_inc(kl_ready, 1)
                for g in range(2):
                    for br in range(2):
                        if br == 0:
                            dve.wait_ge(kl_ready, l * 8 + 2 * g + 2)
                        dve.tensor_copy(KSL[br][(1 - g) * DH:(2 - g) * DH, g, :], KSL[br][g * DH:(g + 1) * DH, g, :])\
                           .then_inc(kl_ready, 1)

                def rotate(h):
                    wait_moved(dve, f"uq{h}", l)
                    if h >= 2:
                        dve.wait_ge(qm_ready, l * MLA_H + h - 1)
                    a, b = rot(h)
                    chain.link(dve.tensor_tensor(a, QM[64:96, h, :], costab[64:96, :], ALU.mult))
                    dve.tensor_tensor(b, QM[96:128, h, :], sintab[96:128, :], ALU.mult).then_inc(qrot_ready, 1)

                rotate(0)
                wait_full(dve, "k2", l)
                release(dve.tensor_copy(kc2[:], bank("k2")[:, 0:2 * NB]), "k2")
                wait_full(dve, "w2", l)
                dve.tensor_copy(vcr[:, 0, :], bank("w2")[:, 0:DH])
                release(dve.tensor_copy(vcr[0:2 * NB, 1, :], bank("w2")[0:2 * NB, DH:2 * DH]), "w2")
                dve.wait_ge(pool_add, l * 2 + 2)
                for k in range(2):
                    for half, s in ((0, pa), (1, pb)):
                        r = slice(half * 64, half * 64 + 64)
                        head, rest = slice(CMP_STRIDE, 2 * CMP_STRIDE), slice(2 * CMP_STRIDE, T + CMP_STRIDE)
                        rc = ct[r, K_RC + k * 16:K_RC + (k + 1) * 16]
                        chain.link(dve.tensor_tensor(pb[r, k, 0:CMP_STRIDE], s[r, k, head], rc, ALU.mult))
                        dve.tensor_tensor(pb[r, k, head], pb[r, k, 0:CMP_STRIDE], up[r, k, head], ALU.subtract)
                        d = dve.scalar_tensor_tensor(out=pb[r, k, rest], in0=s[r, k, rest],
                                                     scalar=ct[r, K_INVW + k:K_INVW + k + 1], in1=up[r, k, rest],
                                                     op0=ALU.mult, op1=ALU.subtract)
                    d.then_inc(pooled_ready, 1)
                for h in range(1, 4):
                    rotate(h)
                for k in range(2):
                    dve.wait_ge(bh_ready, l * B_PL + k + 1)
                    release(dve.scalar_tensor_tensor(out=BL[:, 6 + k, :], in0=bank(f"py{k}"),
                                                     scalar=gl[:, G_PS + k:G_PS + k + 1], in1=f32(BH[:, 6 + k, :]),
                                                     op0=ALU.mult, op1=ALU.subtract), f"py{k}")
                for b in range(2):
                    wait_full(dve, f"cs{b}", l)
                    for t in range(TT):
                        w = 3 * NB
                        d = dve.scalar_tensor_tensor(
                            out=sc[:, t, b:NSA_H:2, :],
                            in0=bank(f"cs{b}")[:, t * w:(t + 1) * w].rearrange("p (h n) -> p h n", n=NB),
                            scalar=1.0,
                            in1=ct[:, K_CM + t * NB:K_CM + (t + 1) * NB].unsqueeze(1).to_broadcast([P, 3, NB]),
                            op0=ALU.mult, op1=ALU.add)
                    release(d, f"cs{b}")
                scv = sc[:].rearrange("p t h n -> p (t h) n")
                wait_moved(dve, "cs0", l)
                wait_moved(dve, "cs1", l)
                chain.link(dve.tensor_reduce(cmx[:], scv, AX_X, ALU.max))
                chain.link(dve.tensor_scalar(cmx[:], cmx[:], NEG_GUARD, None, ALU.max))
                dve.tensor_tensor(scv, scv, cmx[:].unsqueeze(2).to_broadcast([P, TT * NSA_H, NB]), ALU.subtract)\
                   .then_inc(csub_ready, 1)
                rotate(4)
                rotate(5)
                dve.wait_ge(cexp_ready, l + 1)
                chain.link(dve.tensor_reduce(csm[:], scv, AX_X, ALU.add))
                chain.link(dve.tensor_scalar(csm[:], csm[:], TINY, None, ALU.max))
                chain.link(dve.reciprocal(csm[:], csm[:]))
                dve.wait_ge(gates_ready, l + 1)
                csv = csm[:].rearrange("p (t h) -> p t h", t=TT)
                chain.link(dve.tensor_tensor(csv, csv, gates[:, :, 0:GATE_W:3], ALU.mult))
                dve.tensor_tensor(scv, scv, csm[:].unsqueeze(2).to_broadcast([P, TT * NSA_H, NB]), ALU.mult)\
                   .then_inc(cp_ready, 1)
                for t in range(TT):
                    wait_full(dve, f"vm{t}", l)
                    release(dve.tensor_copy(VM[:, t, :], bank(f"vm{t}")[:, 0:MLA_H * VD]), f"vm{t}")

                for s in range(N_UNITS_ATT + 3):
                    if s < N_UNITS_ATT:
                        k = s % 2
                        nsa = s < 2 * NSA_H
                        for b, tiles in (("a", (3,)), ("b", (2, 0)), ("c", (1,))):
                            wait_full(dve, f"s{s}{b}", l)
                            for i in tiles:
                                col = S_PSUM[i]
                                d = dve.tensor_reduce((nms if nsa else nmax)[:, k, i:i + 1],
                                                      psum[:, "abc".index(b), col:col + P * (i + 1)], AX_X, ALU.max,
                                                      negate=True)
                            if b == "b":
                                continue
                            part = slice(3, 4) if b == "a" else slice(0, 3)
                            if not nsa:
                                chain.link(d)
                                d = dve.tensor_scalar(nms[:, k, part], nmax[:, k, part], QK ** -0.5, None, ALU.mult)
                            d.then_inc(max_ready, 1)
                    if s == 2:
                        queries_low(4)
                        queries_low(5)
                    if s == 1:
                        wait_full(dve, "ct1", l)
                        release(dve.tensor_copy(PTc[0:2 * NB, 1, :], bank("ct1")[0:2 * NB, :]), "ct1")
                    if 1 <= s <= N_UNITS_ATT:
                        u = s - 1
                        wait_full(dve, f"t{u}b", l)
                        release(dve.tensor_copy(PT[:, u % 2, 512:1024], psum[:, 4, :]), f"t{u}b")
                    if s < N_UNITS_ATT:
                        for b, part in (("a", slice(3, 4)), ("c", slice(0, 3))):
                            wait_moved(dve, f"s{s}{b}", l)
                            d = dve.reciprocal(fac[:, k, part], ssum[:, k, part])
                            if nsa:
                                chain.link(d)
                                col = 3 * (s // 2) + 1 + s % 2
                                d = dve.tensor_tensor(fac[:, k, part], fac[:, k, part], gates[:, part, col], ALU.mult)
                            d.then_inc(fac_ready, 1)
                    u = s - 3
                    if u >= 0 and (u + 1 == N_UNITS_ATT or PAIR_OF[u + 1] != PAIR_OF[u]):
                        pair = PAIR_OF[u]
                        dve.wait_ge(bh_ready, l * B_PL + 3 + pair)
                        release(dve.tensor_tensor(BL[:, pair, :], bank(f"o{pair}"), f32(BH[:, pair, :]), ALU.subtract),
                                f"o{pair}")
                for m in range(KT):
                    wait_full(dve, f"x{m}", l)
                    release(dve.tensor_tensor(xT[:, m, :], bank(f"x{m}"), xT[:, m, :], ALU.add), f"x{m}")
                    low(m, gl[:, G_LN2 + m:G_LN2 + m + 1], l * 2 * KT + (KT + m + 1))
                residual_norm("ncol2", l * 2 + 1, True, l)
                plain_waits(dve, (moved[PS.bank("nbc2")], PS.before("nbc2", l) + 1))
                with dve.Fori(0, CHUNKS - 1) as c:
                    ff_chunk(l, c, False)
                ff_chunk(l, CHUNKS - 1, True)
                assert chain.n == DVE_PL, chain.n
            chain.layer(DEPTH)
            residual_norm("ncol3", 2 * DEPTH, False)
            for t in range(TT):
                n = 2 * t + 1
                wait_full(dve, f"y{n}")
                dve.tensor_scalar(io[:, t, 512:1024], bank(f"y{n}"), rcol[:, t:t + 1], None, ALU.mult)\
                   .then_inc(y_dve, 1)


def tables():
    c = np.zeros((P, K_W), np.float32)
    p = np.arange(P)
    c[:, K_ID:K_ID + P] = np.eye(P)
    for t in range(TT):
        q = t * P + p
        end = np.arange(NB) * CMP_STRIDE + CMP_LEN - 1
        valid = (end[None, :] <= q[:, None]) & (np.arange(NB)[None, :] < NB - 1)
        c[:, K_CM + t * NB:K_CM + (t + 1) * NB] = np.where(valid, 0.0, NEG)
    for k in range(2):
        for half in range(2):
            w = 2 ** (1 + 2 * k + half)
            rows = slice(half * 64, half * 64 + 64)
            c[rows, K_RC + k * 16:K_RC + (k + 1) * 16] = 1.0 / np.minimum(np.arange(16) + 1, w)
            c[rows, K_INVW + k] = 1.0 / w
    half = ROPE // 2
    inv = np.power(np.float32(10000.0), -(np.arange(half, dtype=np.float32) / np.float32(half)))
    c[:, K_INVF] = inv[p % half]
    c[:, K_SIGN] = np.where(p % ROPE < half, -1.0, 1.0)
    c[:, K_ONE] = 1.0
    tri = np.where(p[None, :] <= p[:, None], 0.0, NEG).astype(np.float32)
    return c, tri


_INS = ["x", "positions", "ln1_g", "w_in", "nsa_cmp_pos", "nsa_cmp_w1", "nsa_cmp_w2", "mla_q_norm", "mla_w_qup",
        "mla_kv_norm", "mla_w_kvup", "pool_w", "pool_scale", "w_out", "ln2_g", "w_ff1", "w_ff2", "final_g"]


def kernel(**inputs):
    import concourse.bacc as _bacc
    from concourse.bass_utils import run_bass_kernel_spmd as _run

    nc = _bacc.Bacc("TRN2", target_bir_lowering=False, num_devices=1)
    arrays = {n: np.ascontiguousarray(inputs[n]) for n in _INS}
    arrays["consts"], arrays["tri"] = tables()
    args = [nc.dram_tensor(f"in_{n}", a.shape, mybir.dt.from_np(a.dtype), kind="ExternalInput").ap()
            for n, a in arrays.items()]
    out = nc.dram_tensor("out_0", (1, T, D), F32, kind="ExternalOutput").ap()
    build(nc, *args, out)
    r = _run(nc, [{f"in_{n}": a for n, a in arrays.items()}], core_ids=[0])
    return r.results[0]["out_0"]
```

```python
from contextlib import ExitStack

import numpy as np

import concourse.bass as bass
from concourse import mybir

ALU = mybir.AluOpType
ACT = mybir.ActivationFunctionType
AX_X = mybir.AxisListType.X
F32 = mybir.dt.float32
F32R = mybir.dt.float32r
BF16 = mybir.dt.bfloat16
I32 = mybir.dt.int32

P = 128
T = 512
TT = T // P
D = 1024
KT = D // P
DEPTH = 2
EPS = 1e-6
NEG = -1.0e30
NEG_GUARD = -1.0e29
ROUND = 1.5 * 2 ** 23
TINY = float(np.finfo(np.float32).tiny)

NSA_H, NSA_G, NSA_HPG, DH = 6, 2, 3, 64
CMP_LEN, CMP_STRIDE, NB = 32, 16, 32
GATE_W = 3 * NSA_H
MLA_H, NOPE, ROPE, VD = 6, 64, 32, 64
QK = NOPE + ROPE
Q_LORA, KV_LORA = 256, 128
POOL_G = 64
D_FF = 4 * D
CHUNKS = D_FF // D

C_Q, C_KV, C_GATE, C_CQ, C_CKV, C_KR, C_POOL = 0, 384, 1152, 1170, 1426, 1554, 1586

IN_UNITS = [
    [(C_CQ, 256)],
    [(C_CKV, 128), (C_GATE, 64), (C_KR, 32)],
    [(C_KV, 256)],
    [(C_KV + 256, 128), (C_KV + 512, 128)],
    [(C_KV + 384, 128), (C_KV + 640, 128)],
    [(C_Q, 256)],
    [(C_Q + 256, 128)],
    [(C_POOL, 256)],
]
IN_WIDTH = [256, 256, 256, 256, 256, 256, 128, 256]
X_ACT = 3
TURN_AT = {1: ("sin", 0), 3: ("cos", 1)}
X_PIECES = 4
U_OUT = len(IN_UNITS)
U_FF = U_OUT + 4
UNITS = U_FF + 8 * CHUNKS

JOBS = [("cq0", 0), ("cq1", 1), ("ncol", 7), ("post", 6), ("ckv", 2), ("nbc", 6), ("kr", 3),
        ("kc", 0), ("vc", 1), ("gt", 5), ("mcol", 7), ("ks", 2), ("kw", 3), ("mbq", 6), ("mbk", 7),
        ("v0", 0), ("v1", 1), ("v2", 2), ("v3", 3), ("q0", 0), ("q1", 1), ("hk", 4), ("hv", 5),
        ("q2", 2), ("u0", 3), ("u1", 0),
        ("uq0", 1), ("uq1", 2), ("k2", 4), ("w2", 5), ("uq2", 3), ("uq3", 0), ("cs0", 6), ("cs1", 7),
        ("uq4", 1), ("uq5", 2), ("kn0", 3), ("kn1", 0), ("kn2", 1),
        ("vm0", 2), ("vm1", 3), ("vm2", 0), ("vm3", 1)]
N_UNITS_ATT = 2 * NSA_H + MLA_H
UNIT = [(2 * _p + _h, _b) for _p in range(NSA_H // 2) for _b in range(2) for _h in range(2)] +\
       [(_h, 0) for _h in range(MLA_H)]
PAIR_OF = [_u // 4 for _u in range(2 * NSA_H)] + [NSA_H // 2 + _h // 2 for _h in range(MLA_H)]
ROTATE_AT = [3 + 2 * h for h in range(MLA_H)]
POOL_AT = (2, 4)
for _s in range(N_UNITS_ATT + 3):
    if _s < N_UNITS_ATT:
        JOBS += [(f"s{_s}a", 0), (f"s{_s}b", 1), (f"s{_s}c", 2)]
    if _s == 0:
        JOBS += [("ct0", 4), ("ct1", 5)]
    if 2 <= _s < N_UNITS_ATT + 2:
        JOBS += [(f"t{_s - 2}a", 3), (f"t{_s - 2}b", 4), (f"t{_s - 2}c", 5)]
    if _s in POOL_AT:
        JOBS += [(f"py{POOL_AT.index(_s)}", 7)]
    if _s >= 4 and _s % 2 == 0 and (_s == 4 or PAIR_OF[_s - 4] != PAIR_OF[_s - 5]):
        JOBS += [(f"o{PAIR_OF[_s - 4]}", 6 + PAIR_OF[_s - 4] % 2)]
JOBS += [(f"x{m}", m % 4) for m in range(KT)]
JOBS += [("ncol2", 7), ("nbc2", 6)]
FF_JOBS = [(f"f{m}", m % 4) for m in range(KT)] + [(f"g{m}", m % 4) for m in range(KT)]
PRE_JOBS = [("gain", 7), ("sin", 7), ("cos", 7)] + [(f"p{m}", m % 7) for m in range(KT)] + [("par", 7)]
POST_JOBS = [("ncol3", 7)] + [(f"y{n}", n) for n in range(2 * TT)]

PAR0 = KT
PAR_L = 2 * KT + 5
G_LN2, G_NEXT, G_QN, G_KVN, G_PS = 0, KT, 2 * KT, 2 * KT + 2, 2 * KT + 3

K_ID, K_CM, K_RC, K_INVW, K_INVF, K_SIGN, K_ONE = 0, 128, 256, 288, 290, 306, 307
K_W = 308

S_TILES = [(3, 0, 0, 0), (2, 1, 0, 512), (0, 1, 384, 896), (1, 2, 0, 1024)]
S_PART = {"a": slice(3, 4), "bc": slice(0, 3)}
S_COL = {i: c for i, _, _, c in S_TILES}
T_TILES = [(0, 0, 0, 0), (1, 1, 0, 512), (3, 1, 384, 896), (2, 2, 0, 1024)]
T_COL = {j: c for j, _, _, c in T_TILES}
PW = 1280


def bank_counts(jobs):
    return [sum(b == k for _, b in jobs) for k in range(8)]


class Psum:

    def __init__(self):
        self.pre, self.body = bank_counts(PRE_JOBS), bank_counts(JOBS)
        self.ff = bank_counts(FF_JOBS)
        self.layer = [a + CHUNKS * f for a, f in zip(self.body, self.ff)]
        self.place = {}
        for jobs, base, kind in ((PRE_JOBS, [0] * 8, "pre"), (JOBS, self.pre, "layer"),
                                 (FF_JOBS, [a + b for a, b in zip(self.pre, self.body)], "ff"),
                                 (POST_JOBS, [a + DEPTH * b for a, b in zip(self.pre, self.layer)], "post")):
            seen = list(base)
            for name, b in jobs:
                self.place[name] = (b, seen[b], kind)
                seen[b] += 1

    def bank(self, name):
        return self.place[name][0]

    def before(self, name, l=0, c=0):
        b, n, kind = self.place[name]
        if kind in ("pre", "post"):
            return n
        v = l * self.layer[b] + n
        return v + c * self.ff[b] if kind == "ff" else v


PS = Psum()


class Chain:

    def __init__(self, eng, sem, per_layer, base=0):
        self.eng, self.sem, self.per, self.base, self.n, self.l = eng, sem, per_layer, base, 0, 0

    def layer(self, l):
        self.n, self.l = 0, l

    def link(self, ins):
        ins.then_inc(self.sem, 1)
        self.n += 1
        self.eng.wait_ge(self.sem, self.l * self.per + self.base + self.n)


def build(nc, x, positions, ln1_g, w_in, nsa_cmp_pos, nsa_cmp_w1, nsa_cmp_w2, mla_q_norm, mla_w_qup,
          mla_kv_norm, mla_w_kvup, pool_w, pool_scale, w_out, ln2_g, w_ff1, w_ff2, final_g,
          consts, tri, out):
    with ExitStack() as ctx:
        top = [-(-nc.sbuf_base // 32) * 32]

        def at_(name, shape, dt, offset):
            return nc.alloc_sbuf_tensor_at(name, shape, dt, offset=offset)

        def size(shape, dt):
            return int(np.prod(shape[1:])) * (2 if dt == BF16 else 4)

        def sb(name, shape, dt=F32):
            t = at_(name, shape, dt, top[0])
            t_off[name] = top[0]
            top[0] += -(-size(shape, dt) // 32) * 32
            return t

        t_off = {}

        def sem(name):
            return ctx.enter_context(nc.semaphore(name))

        xT = sb("xT", [P, KT, T])
        XH, XL = sb("XH", [P, KT, T], F32R), sb("XL", [P, KT, T], F32R)
        BH, BL = sb("BH", [P, KT, T], F32R), sb("BL", [P, KT, T], F32R)
        raw = sb("raw", [P, 2, KT, 256])
        WH, WL = sb("WH", [P, 2, KT, 256], F32R), sb("WL", [P, 2, KT, 256], F32R)
        io = sb("io", [P, TT, D])
        PT = sb("PT", [P, 2, PW])
        rs = sb("rs", [P, T])
        sqt = sb("sqt", [P, 3, T])
        costab, sintab = sb("costab", [P, T]), sb("sintab", [P, T])
        ct = sb("ct", [P, K_W])
        identb, trib = sb("identb", [P, P], BF16), sb("trib", [P, P], BF16)
        qT = sb("qT", [P, 3, T])
        KSH = sb("KSH", [P, 2, 2, T], F32R)
        VN = sb("VN", [P, TT, 256])
        gates = sb("gates", [P, TT, GATE_W])
        cq, ckv = sb("cq", [P, 2, T]), sb("ckv", [P, T])
        kcv = sb("kcv", [P, 2, T + CMP_STRIDE])
        up = sb("up", [P, 2, T + CMP_STRIDE])
        PTc = sb("PTc", [P, 2, T])
        KB = sb("KB", [P, NSA_H // 2, 2 * NB])
        vcr = sb("vcr", [P, 2, DH])
        pos2 = sb("pos2", [P, 2 * CMP_LEN])
        pw = sb("pw", [P, 2, P])
        params, gl = sb("params", [P, PAR0 + DEPTH * PAR_L]), sb("gl", [P, PAR_L])
        rcol = sb("rcol", [P, 12])
        na, nt, ni = sb("na", [P, 8]), sb("nt", [P, 8]), sb("ni", [P, 8], I32)
        nmax, nms, ssum, fac = (sb(n, [P, 3, TT]) for n in ("nmax", "nms", "ssum", "fac"))
        cmx, csm = sb("cmx", [P, 4 * NSA_H]), sb("csm", [P, 4 * NSA_H])
        assert top[0] <= nc.sbuf_usable_end, (top[0], nc.sbuf_usable_end)

        def over(name, shape, dt, host, skip=0):
            return at_(name, shape, dt, t_off[host] + skip)

        QM = over("QM", [P, MLA_H, T], F32, "XH")
        KM = over("KM", [P, MLA_H, T], F32, "XL")
        wq = over("wq", [P, 2, MLA_H, P], F32, "BH")
        wkv = over("wkv", [P, 2, MLA_H, 64], F32, "BH", 6144)
        w2 = over("w2", [DH, 3, DH], F32, "BH", 9216)
        KSL = [over(f"KSL{b}", [P, 2, T], F32R, t, 6 * T * 4) for b, t in enumerate(("XH", "XL"))]
        QS = [over(f"QS{h}", [P, T], F32R, "BL", h * T * 4) for h in range(4)] +\
             [over(f"QS{h}", [P, T], F32R, "BH", (h - 2) * T * 4) for h in range(4, NSA_H)]
        kraw = over("kraw", [P, 2, T], F32, "io")
        bcmp = over("bcmp", [P, 2, 16, 2 * NB], F32, "BL")
        sc = over("sc", [P, TT, NSA_H, NB], F32, "BL", 8192)
        hx, hg = (over(n, [DH, 2, 2 * NB], F32, "BL", 11264 + 512 * k) for k, n in enumerate(["hx", "hg"]))
        pr01, pr2 = over("pr01", [P, 2, PW], F32, "io"), over("pr2", [P, PW], F32, "cq")
        pr = [pr01[:, 0, :], pr01[:, 1, :], pr2[:]]
        VM = over("VM", [P, TT, MLA_H * VD], F32, "io", 10240)
        pa = over("pa", [P, 2, T + CMP_STRIDE], F32, "PT", PW * 4)
        pb = over("pb", [P, 2, T + CMP_STRIDE], F32, "sqt")
        prs = over("prs", [2 * CMP_LEN, P], F32, "io", 9024)
        w1 = over("w1", [P, 2, 16, DH], F32, "PT")
        krz, krt = over("krz", [P, T], F32, "PTc"), over("krt", [P, T], F32, "PTc", 2048)
        relu, asq = (over(n, [P, 2, T], F32, "io", k * 4096) for k, n in enumerate(["relu", "asq"]))
        prow = over("prow", [P, P], F32, "PTc")
        trif = over("trif", [P, P], F32, "PTc", 512)
        HALF = ROPE // 2
        posi, posf = over("posi", [P, TT], I32, "KSH"), over("posf", [P, TT], F32, "KSH", 64)
        ang, turns, arg = (over(n, [P, s, TT, HALF], F32, "KSH", o) for n, s, o in
                           (("ang", 1, 512), ("turns", 2, 1024), ("arg", 2, 2048)))
        sincos = over("sincos", [P, 2, TT, P], F32, "KSH", 4096)
        identr = over("identr", [P, P], F32R, "KSH")
        ident = ct[:, K_ID:K_ID + P]
        ones = ct[:, K_ONE:K_ONE + 1]

        psum = ctx.enter_context(nc.psum_tensor("psum", [P, 8, 512], F32))

        def f32(ap):
            return ap.bitcast(F32)

        def rot(h):
            if h % 2:
                return up[64:96, 0, CMP_STRIDE:], up[64:96, 1, CMP_STRIDE:]
            return kcv[64:96, 0, 0:T], kcv[64:96, 1, 0:T]

        full = [sem(f"bank_full{b}") for b in range(8)]
        moved = [sem(f"bank_moved{b}") for b in range(8)]
        x_loaded = [sem(f"x_loaded{k}") for k in range(X_PIECES)]
        gain_loaded, par_loaded, const_loaded = sem("gain_loaded"), sem("par_loaded"), sem("const_loaded")
        small_loaded = sem("small_loaded")
        raw_loaded = [sem(f"raw_loaded{s}") for s in range(2)]
        w_lo0 = sem("w_lo0")
        w_hi, w_lo = sem("w_hi"), sem("w_lo")
        kr_cols = sem("kr_cols")
        wq_cols = sem("wq_cols")
        zeros_set, masks_set = sem("zeros_set"), sem("masks_set")
        gl_ready = sem("gl_ready")
        xh_ready, xl_ready = sem("xh_ready"), sem("xl_ready")
        sq_ready, sq_added = sem("sq_ready"), sem("sq_added")
        rcol_ready, diag_ready = sem("rcol_ready"), sem("diag_ready")
        msq_ready, mdiag_ready = sem("msq_ready"), sem("mdiag_ready")
        kh_ready, kl_ready = sem("kh_ready"), sem("kl_ready")
        qh_ready, ql_ready = sem("qh_ready"), sem("ql_ready")
        gates_ready = sem("gates_ready")
        krot_ready, kr_spread = sem("krot_ready"), sem("kr_spread")
        bcmp_ready = sem("bcmp_ready")
        gelu_arg, gelu_exp, hg_ready = sem("gelu_arg"), sem("gelu_exp"), sem("hg_ready")
        pool_add, pooled_ready = sem("pool_add"), sem("pooled_ready")
        qrot_ready, qm_ready = sem("qrot_ready"), sem("qm_ready")
        csub_ready, cexp_ready, cp_ready = sem("csub_ready"), sem("cexp_ready"), sem("cp_ready")
        max_ready, fac_ready, p_ready = sem("max_ready"), sem("fac_ready"), sem("p_ready")
        bh_ready = sem("bh_ready")
        bl_ready = sem("bl_ready")
        asq_ready = sem("asq_ready")
        dve_step, pool_step = sem("dve_step"), sem("pool_step")
        trig_arg, sin_ready = sem("trig_arg"), sem("sin_ready")
        identr_ready, y_act, y_dve, stored = sem("identr_ready"), sem("y_act"), sem("y_dve"), sem("stored")

        def plain_waits(eng, *waits):
            values = [(s, eng.to_reg(v)) for s, v in waits]
            eng.wait_ge(const_loaded, 48)
            for s, v in values:
                eng.wait_ge(s, v)

        def free_before(name, l):
            return moved[PS.bank(name)], PS.before(name, l)

        def wait_full(eng, name, l=0, c=0):
            eng.wait_ge(full[PS.bank(name)], PS.before(name, l, c) + 1)

        def wait_moved(eng, name, l=0, c=0):
            eng.wait_ge(moved[PS.bank(name)], PS.before(name, l, c) + 1)

        def release(ins, name):
            ins.then_inc(moved[PS.bank(name)], 1)

        B_PL = KT + KT * CHUNKS
        B_ORDER = [6, 7, 0, 1, 2, 3, 4, 5]
        NSMALL = 15
        DVE_PRE, DVE_PL = 8, 99
        POOL_PL = 5

        def split_counts(n, l, c=0):
            hi, lo = (1, 1) if n < 0 else (n + 4, n + 2)
            return (w_hi, l * HI_PL + c * 8 + hi), (w_lo, l * UNITS + c * 8 + lo)

        HI_PL = UNITS + 2

        def raw_count(n):
            return sum(len(IN_UNITS[k]) if k < U_OUT else 1 for k in range(n % 2, n + 1, 2))

        RAW_PL = [raw_count(UNITS - 2), raw_count(UNITS - 1)]

        block = ctx.enter_context(nc.Block())

        @block.sync
        def _(sp):
            sp.dma_start(ct[:], consts).then_inc(const_loaded, 16)
            sp.dma_start(posi[:], positions[0].rearrange("(p t) -> p t", p=P)).then_inc(const_loaded, 16)
            sp.dma_start(trif[:], tri).then_inc(const_loaded, 16)

            def par(row, src, loaded):
                r = src.rearrange("(r p) -> r p", p=P)
                sp.dma_start(prow[row:row + r.shape[0], :], r).then_inc(loaded, 16)

            par(0, ln1_g[0], gain_loaded)
            for k in range(X_PIECES):
                cols = slice(k * D // X_PIECES, (k + 1) * D // X_PIECES)
                sp.dma_start(io[:, :, cols], x[0, :, cols].rearrange("(t p) d -> p t d", p=P)).then_inc(x_loaded[k], 16)

            for l in range(DEPTH):
                b = PAR0 + PAR_L * l
                par(b + G_LN2, ln2_g[l], par_loaded)
                par(b + G_NEXT, ln1_g[l + 1] if l + 1 < DEPTH else final_g, par_loaded)
                par(b + G_QN, mla_q_norm[l], par_loaded)
                par(b + G_KVN, mla_kv_norm[l], par_loaded)
                par(b + G_PS, pool_scale[l], par_loaded)

            def load(n, l, pieces):
                plain_waits(sp, *split_counts(n - 2, l), *([(w_lo0, l * 2 + 2)] if n == 2 else []))
                col = 0
                for src, width in pieces:
                    sp.dma_start(raw[:, n % 2, :, col:col + width],
                                 src.rearrange("(k p) n -> p k n", p=P)).then_inc(raw_loaded[n % 2], 16)
                    col += width

            def load_in(n, l):
                load(n, l, [(w_in[l, :, a:a + w], w) for a, w in IN_UNITS[n]])

            def load_ff(l, c):
                for u in range(8):
                    plain_waits(sp, *split_counts(U_FF + u - 2, l, c))
                    if u < 4:
                        src = w_ff1[l, :, bass.ds(c * D + 256 * u, 256)]
                    else:
                        src = w_ff2[l, bass.ds(c * D, D), 256 * (u - 4):256 * (u - 3)]
                    sp.dma_start(raw[:, u % 2, :, :], src.rearrange("(k p) n -> p k n", p=P))\
                      .then_inc(raw_loaded[u % 2], 16)

            with sp.Fori(0, DEPTH) as l:
                load_in(0, l)
                load_in(1, l)
                b = PS.bank("g7")
                plain_waits(sp, (full[b], l * PS.layer[b] + PS.pre[b]))
                for g in range(2):
                    sp.dma_start(prs[:, g * DH:(g + 1) * DH],
                                 nsa_cmp_pos[l].rearrange("v l d -> (v l) d")).then_inc(small_loaded, 16)
                    sp.dma_start(w1[:, g, :, :], nsa_cmp_w1[l, g].rearrange("(a b) d e -> (b d) a e", b=2))\
                      .then_inc(small_loaded, 16)
                    sp.dma_start(wq[:, g, :, 0:QK],
                                 mla_w_qup[l, g * P:(g + 1) * P, :].rearrange("p (h c) -> p h c", c=QK))\
                      .then_inc(small_loaded, 16)
                for k, g in enumerate((0, 0, 1)):
                    sp.dma_start(w2[:, k, :], nsa_cmp_w2[l, g]).then_inc(small_loaded, 16)
                for s in range(2):
                    sp.dma_start(wkv[:, s, :, :], mla_w_kvup[l].rearrange("p (h s c) -> p s h c", s=2, c=64)[:, s, :, :])\
                      .then_inc(small_loaded, 16)
                sp.wait_ge(zeros_set, 1)
                for g in range(4):
                    r = (g % 2) * POOL_G
                    sp.dma_start(pw[r:r + POOL_G, g // 2, r:r + POOL_G], pool_w[l, g]).then_inc(small_loaded, 16)
                for n in range(2, U_OUT):
                    load_in(n, l)
                for m in range(4):
                    load(U_OUT + m, l, [(w_out[l, :, 256 * m:256 * (m + 1)], 256)])
                with sp.Fori(0, CHUNKS) as c:
                    load_ff(l, c)
            for t in range(TT):
                sp.wait_ge(y_act, t + 1)
                sp.wait_ge(y_dve, t + 1)
                sp.dma_start(out[0, t * P:(t + 1) * P, :], io[:, t, :]).then_inc(stored, 16)
            sp.wait_ge(stored, 16 * TT)

        @block.tensor
        def _(pe):
            def begin(name, l=0, c=0):
                pe.wait_ge(moved[PS.bank(name)], PS.before(name, l, c))
                return psum[:, PS.bank(name), :]

            def done(mm, name):
                mm.then_inc(full[PS.bank(name)], 1)

            def three(o, wh, wl, h, lo, first, last):
                pe.matmul(o, wh, h, start=first, stop=False)
                pe.matmul(o, wl, h, start=False, stop=False)
                return pe.matmul(o, wh, lo, start=False, stop=last)

            def unit_split(n, l, c=0):
                for s, v in split_counts(n, l, c):
                    pe.wait_ge(s, v)

            def dense(name, slot, half, l, c=0, H=XH, L=XL, tiles=None, order=range(KT), first=True, last=True):
                o = begin(name, l, c) if first else psum[:, PS.bank(name), :]
                for n, k in enumerate(order):
                    if tiles is not None:
                        tiles(k)
                    cols = slice(half * P, (half + 1) * P)
                    mm = three(o, WH[:, slot, k, cols], WL[:, slot, k, cols], H[:, k, :], L[:, k, :],
                               first and n == 0, last and n == len(order) - 1)
                if last:
                    done(mm, name)

            def columns(name, l=0):
                o = begin(name, l)
                for t in range(TT):
                    mm = pe.matmul(o[:, t:t + 1], rs[:, t * P:(t + 1) * P], ones, start=True, stop=True)
                done(mm, name)

            def spread(name, k, l=0):
                o = begin(name, l)
                done(pe.matmul(o, ones.to_broadcast([P, P]), sqt[:, k, :], start=True, stop=True), name)

            pe.wait_ge(const_loaded, 48)

            def turned(name, k):
                pe.wait_ge(sin_ready, k + 1)
                o = begin(name)
                for t in range(TT):
                    mm = pe.transpose(o[:, t * P:(t + 1) * P], sincos[:, k, t, :], ident)
                done(mm, name)

            pe.wait_ge(gain_loaded, 16)
            done(pe.transpose(begin("gain")[:, 0:PAR0], prow[0:PAR0, :], ct[0:PAR0, K_ID:K_ID + PAR0]), "gain")
            for m in range(KT):
                if m in TURN_AT:
                    turned(*TURN_AT[m])
                pe.wait_ge(x_loaded[m * X_PIECES // KT], 16)
                o = begin(f"p{m}")
                for t in range(TT):
                    mm = pe.transpose(o[:, t * P:(t + 1) * P], io[:, t, m * P:(m + 1) * P], ident)
                done(mm, f"p{m}")
            pe.wait_ge(par_loaded, 16 * 5 * DEPTH)
            n = PAR0 + DEPTH * PAR_L
            done(pe.transpose(begin("par")[:, 0:n], prow[0:n, :], ct[0:n, K_ID:K_ID + n]), "par")

            def attention(l):
                def operands(u):
                    if u < 2 * NSA_H:
                        h, br = UNIT[u]
                        g = h // NSA_HPG
                        return QS[h], (KSH[:, br, g, :], KSL[br][:, g, :])
                    h = u - 2 * NSA_H
                    return QM[0:QK, h, :], (KM[0:QK, h, :],)

                def scores(u):
                    q, keys = operands(u)
                    if u == 0:
                        pe.wait_ge(kh_ready, l * 4 + 4)
                        pe.wait_ge(kl_ready, l * 8 + 8)
                    if u < 2 * NSA_H and UNIT[u][1] == 0:
                        pe.wait_ge(ql_ready, l * NSA_H + UNIT[u][0] + 1)
                    if u >= 2 * NSA_H:
                        pe.wait_ge(qm_ready, l * MLA_H + u - 2 * NSA_H + 1)
                    if u == 2 * NSA_H:
                        pe.wait_ge(kr_spread, l + 1)
                        for t in range(TT):
                            wait_moved(pe, f"vm{t}", l)
                    for i, b, col, _ in S_TILES:
                        name = f"s{u}{'abc'[b]}"
                        o = begin(name, l) if col == 0 else psum[:, b, :]
                        n = P * (i + 1)
                        for m, k in enumerate(keys):
                            pe.matmul(o[:, col:col + n], q[:, i * P:(i + 1) * P], k[:, 0:n], start=m == 0, stop=False)
                        mm = pe.matmul(o[:, col + n - P:col + n], identb[:], trib[:], start=False, stop=True)
                        if col or b != 1:
                            done(mm, name)

                def transposes(u):
                    pe.wait_ge(p_ready, l * 4 * N_UNITS_ATT + 4 * (u + 1))
                    for j, b, col, _ in T_TILES:
                        name = f"t{u}{'abc'[b]}"
                        o = begin(name, l) if col == 0 else psum[:, 3 + b, :]
                        for i in range(j, TT):
                            mm = pe.transpose(o[:, col + (i - j) * P:col + (i - j + 1) * P],
                                              pr[u % 3][:, S_COL[i] + j * P:S_COL[i] + (j + 1) * P], ident)
                        if col or b != 1:
                            done(mm, name)

                def values(first_unit):
                    units = (first_unit, first_unit + 1)
                    pair = PAIR_OF[first_unit]
                    name = f"o{pair}"
                    if first_unit == 0 or PAIR_OF[first_unit - 1] != pair:
                        begin(name, l)
                    for b in "abc":
                        wait_moved(pe, f"t{units[1]}{b}", l)
                    nsa = first_unit < 2 * NSA_H
                    for j in range(TT):
                        for u in units:
                            h, br = UNIT[u]
                            r = (h % 2) * 64
                            o = psum[r:r + 64, PS.bank(name), :]
                            if nsa:
                                g = br * NSA_G + h // NSA_HPG
                                v = VN[:, j, g * DH:(g + 1) * DH]
                            else:
                                v = VM[:, j, h * VD:(h + 1) * VD]
                            start, stop = j == 0 and br == 0, j == TT - 1 and (br == 1 or not nsa)
                            if nsa and start:
                                q, b = (h % 4) * NB, h // 4
                                pe.matmul(o, vcr[q:q + NB, b, :], PTc[q:q + NB, b, :], start=True, stop=False)
                                start = False
                            n = T - j * P
                            mm = pe.matmul(o[:, j * P:T], v, PT[:, u % 2, T_COL[j]:T_COL[j] + n],
                                           start=start, stop=stop)
                    if u + 1 == N_UNITS_ATT or PAIR_OF[u + 1] != pair:
                        done(mm, name)

                for s in range(N_UNITS_ATT + 3):
                    if s < N_UNITS_ATT:
                        scores(s)
                    if s == 0:
                        pe.wait_ge(cp_ready, l + 1)
                        pe.wait_ge(kr_spread, l + 1)
                        for b, n in ((0, 4), (1, 2)):
                            plain_waits(pe, free_before(f"ct{b}", l))
                            o = psum[:, PS.bank(f"ct{b}"), :]
                            for t in range(TT):
                                mm = pe.transpose(o[0:n * NB, t * P:(t + 1) * P],
                                                  sc[:, t, 4 * b:4 * b + n, :].rearrange("p h n -> p (h n)"), ident)
                            done(mm, f"ct{b}")
                    if s == N_UNITS_ATT:
                        unit_split(U_OUT, l)
                        dense("x0", 0, 0, l, 0, BH, BL, lambda k: mixed(k, l), B_ORDER[:3], last=False)
                    if s % 2 == 0 and s >= 4:
                        values(s - 4)
                    if 2 <= s < N_UNITS_ATT + 2:
                        transposes(s - 2)
                    if s == N_UNITS_ATT + 1:
                        dense("x0", 0, 0, l, 0, BH, BL, lambda k: mixed(k, l), B_ORDER[3:6], first=False, last=False)
                    if s in POOL_AT:
                        k = POOL_AT.index(s)
                        pe.wait_ge(pooled_ready, l * 2 + k + 1)
                        done(pe.matmul(begin(f"py{k}", l), pw[:, k, :], pb[:, k, CMP_STRIDE:], start=True, stop=True),
                             f"py{k}")

            def hidden(k, l, c):
                pe.wait_ge(bh_ready, l * B_PL + c * KT + (KT + k + 1))
                pe.wait_ge(bl_ready, l * (KT * CHUNKS) + c * KT + (k + 1))

            def mixed(k, l):
                pe.wait_ge(bh_ready, l * B_PL + B_ORDER.index(k) + 1)
                wait_moved(pe, f"o{k}" if k < 6 else f"py{k - 6}", l)

            def gained(k, l):
                pe.wait_ge(xh_ready, l * 2 * KT + (k + 1))
                pe.wait_ge(xl_ready, l * 2 * KT + (k + 1))

            def ff_chunk(l, c):
                for m in range(2, KT):
                    if m % 2 == 0:
                        unit_split(U_FF + m // 2, l, c)
                    dense(f"f{m}", (m // 2) % 2, m % 2, l, c)
                for m in range(KT):
                    if m % 2 == 0:
                        unit_split(U_FF + 4 + m // 2, l, c)
                    dense(f"g{m}", (m // 2) % 2, m % 2, l, c, BH, BL,
                          (lambda k: hidden(k, l, c)) if m == 0 else None)

            with pe.Fori(0, DEPTH) as l:
                def first_tile(k):
                    if k % (KT // 2) == 0:
                        pe.wait_ge(w_lo0, l * 2 + (1 + k // (KT // 2)))
                    gained(k, l)

                dense("cq0", 0, 0, l, tiles=first_tile)
                unit_split(0, l)
                dense("cq1", 0, 1, l)
                pe.wait_ge(sq_added, (l * 2 + 1) * KT)
                columns("ncol", l)
                plain_waits(pe, (small_loaded, (l + 1) * (16 * NSMALL)), free_before("post", l))
                done(pe.transpose(psum[:, PS.bank("post"), 0:2 * CMP_LEN], prs[:, :], ct[0:2 * CMP_LEN, K_ID:K_ID + 2 * CMP_LEN]),
                     "post")
                unit_split(1, l)
                dense("ckv", 1, 0, l)
                pe.wait_ge(diag_ready, l * 2 + 1)
                spread("nbc", 0, l)
                dense("kr", 1, 1, l)
                unit_split(2, l)
                dense("kc", 0, 0, l)
                dense("vc", 0, 1, l)
                wait_moved(pe, "kr", l)
                plain_waits(pe, free_before("gt", l))
                for t in range(TT):
                    mm = pe.transpose(psum[:, PS.bank("gt"), t * GATE_W:(t + 1) * GATE_W],
                                      krz[0:GATE_W, t * P:(t + 1) * P], ct[0:GATE_W, K_ID:K_ID + GATE_W])
                done(mm, "gt")
                pe.wait_ge(msq_ready, l * 3 + 3)
                o = begin("mcol", l)
                for t in range(TT):
                    cols = slice(t * P, (t + 1) * P)
                    pe.matmul(o[:, t:t + 1], sqt[:, 0, cols], ones, start=True, stop=False)
                    pe.matmul(o[:, t:t + 1], sqt[:, 1, cols], ones, start=False, stop=True)
                for t in range(TT):
                    mm = pe.matmul(o[:, TT + t:TT + t + 1], sqt[:, 2, t * P:(t + 1) * P], ones, start=True, stop=True)
                done(mm, "mcol")
                unit_split(3, l)
                dense("ks", 1, 0, l)
                dense("kw", 1, 1, l)
                pe.wait_ge(mdiag_ready, l + 1)
                spread("mbq", 1, l)
                spread("mbk", 2, l)
                unit_split(4, l)
                for t in range(TT):
                    o = begin(f"v{t}", l)[:, 0:256]
                    cols = slice(t * P, (t + 1) * P)
                    for k in range(KT):
                        pe.matmul(o, XH[:, k, cols], WH[:, 0, k, :], start=(k == 0), stop=False)
                        pe.matmul(o, XH[:, k, cols], WL[:, 0, k, :], start=False, stop=False)
                        mm = pe.matmul(o, XL[:, k, cols], WH[:, 0, k, :], start=False, stop=(k == KT - 1))
                    done(mm, f"v{t}")
                unit_split(5, l)
                dense("q0", 1, 0, l)
                dense("q1", 1, 1, l)
                pe.wait_ge(bcmp_ready, l * 8 + 8)
                for v, name in enumerate(("hk", "hv")):
                    o = begin(name, l)
                    for a in range(16):
                        mm = pe.matmul(o[0:DH, 0:2 * NB], w1[:, v, a, :], bcmp[:, v, a, :], start=(a == 0), stop=(a == 15))
                    done(mm, name)
                unit_split(6, l)
                dense("q2", 0, 0, l)
                unit_split(7, l)
                dense("u0", 1, 0, l)
                dense("u1", 1, 1, l)

                def up_q(h):
                    o = begin(f"uq{h}", l)
                    for k in range(2):
                        mm = pe.matmul(o, wq[:, k, h, :], cq[:, k, :], start=(k == 0), stop=(k == 1))
                    done(mm, f"uq{h}")

                pe.wait_ge(wq_cols, l + 1)
                wait_moved(pe, "mbq", l)
                up_q(0)
                up_q(1)
                pe.wait_ge(hg_ready, l + 1)
                done(pe.matmul(begin("k2", l)[:, 0:2 * NB], w2[:, 0:2, :].rearrange("p a f -> p (a f)"), hg[:, 0, :],
                               start=True, stop=True), "k2")
                plain_waits(pe, free_before("w2", l))
                for h in range(NSA_H):
                    q, b, g = (h % 4) * NB, h // 4, h // NSA_HPG
                    mm = pe.matmul(psum[q:q + NB, PS.bank("w2"), b * DH:(b + 1) * DH], hg[:, 1, g * NB:(g + 1) * NB],
                                   w2[:, 2, :], start=True, stop=True)
                done(mm, "w2")
                up_q(2)
                up_q(3)
                wait_moved(pe, "k2", l)
                wait_moved(pe, "q2", l)
                for b in range(2):
                    o = begin(f"cs{b}", l)
                    for t in range(2 * b, 2 * b + 2):
                        for pair in range(NSA_H // 2):
                            col = ((t % 2) * NSA_H + 2 * pair) * NB
                            mm = pe.matmul(o[:, col:col + 2 * NB], qT[:, pair, t * P:(t + 1) * P], KB[:, pair, :],
                                           start=True, stop=True)
                    done(mm, f"cs{b}")
                up_q(4)
                up_q(5)
                wait_moved(pe, "mbk", l)
                for p in range(3):
                    w = wkv[:, 0, 2 * p:2 * p + 2, :].rearrange("p h c -> p (h c)")
                    done(pe.matmul(begin(f"kn{p}", l), w, ckv[:], start=True, stop=True), f"kn{p}")
                for t in range(TT):
                    w = wkv[:, 1, :, :].rearrange("p h c -> p (h c)")
                    done(pe.matmul(begin(f"vm{t}", l)[:, 0:MLA_H * VD], ckv[:, t * P:(t + 1) * P], w,
                                   start=True, stop=True), f"vm{t}")
                attention(l)
                dense("x1", 0, 1, l, 0, BH, BL, lambda k: mixed(k, l), B_ORDER[:7], last=False)
                dense("x0", 0, 0, l, 0, BH, BL, lambda k: mixed(k, l), B_ORDER[6:], first=False)
                dense("x1", 0, 1, l, 0, BH, BL, None, B_ORDER[7:], first=False)
                for m in range(2, KT):
                    if m % 2 == 0:
                        unit_split(U_OUT + m // 2, l)
                    dense(f"x{m}", (m // 2) % 2, m % 2, l, 0, BH, BL)
                unit_split(U_FF, l)
                dense("f0", 0, 0, l, tiles=lambda k: gained(KT + k, l))
                pe.wait_ge(sq_added, (l * 2 + 2) * KT)
                columns("ncol2", l)
                dense("f1", 0, 1, l)
                pe.wait_ge(diag_ready, l * 2 + 2)
                spread("nbc2", 0, l)
                with pe.Fori(0, CHUNKS - 1) as c:
                    ff_chunk(l, c)
                    unit_split(U_FF, l, c + 1)
                    dense("f0", 0, 0, l, c + 1)
                    dense("f1", 0, 1, l, c + 1)
                ff_chunk(l, CHUNKS - 1)

            def back(n):
                t, half = n // 2, n % 2
                pe.wait_ge(xl_ready, 2 * DEPTH * KT + (half + 1) * KT // 2)
                o = begin(f"y{n}")
                for m in range(4):
                    k = half * 4 + m
                    cols = slice(m * P, (m + 1) * P)
                    pe.matmul(o[:, cols], XH[:, k, t * P:(t + 1) * P], identr[:], start=True, stop=False)
                    mm = pe.matmul(o[:, cols], XL[:, k, t * P:(t + 1) * P], identr[:], start=False, stop=True)
                done(mm, f"y{n}")

            pe.wait_ge(identr_ready, DEPTH)
            for n in (0, 2, 4):
                back(n)
            pe.wait_ge(sq_added, (2 * DEPTH + 1) * KT)
            columns("ncol3")
            for n in (6, 1, 3, 5, 7):
                back(n)

        @block.scalar
        def _(act):
            def copy(o, i, **kw):
                return act.activation(o, i, ACT.Copy, **kw)

            def split_hi(n, l, job, c=None):
                s = n % 2
                if c is None:
                    act.wait_ge(raw_loaded[s], l * (16 * RAW_PL[s]) + 16 * raw_count(n))
                else:
                    act.wait_ge(raw_loaded[s], l * (16 * RAW_PL[s]) + c * 64 + 16 * raw_count(n))
                if job is not None:
                    wait_full(act, *job)
                w = IN_WIDTH[n] if n < U_OUT else 256
                if n == 1:
                    act.wait_ge(kr_cols, l * 2 + 2)
                if n == 0:
                    for k in range(0, KT, KT // 2):
                        copy(WH[:, s, k:k + KT // 2, 0:P], raw[:, s, k:k + KT // 2, 0:P]).then_inc(w_hi, 1)
                    square(KT - 1, l * 2)
                a = P if n == 0 else 0
                copy(WH[:, s, :, a:w], raw[:, s, :, a:w]).then_inc(w_hi, 1)

            def prep(m, norm, gain, odd=False):
                copy(XH[:, m, :], xT[:, m, :], scale=gain).then_inc(xh_ready, 1)
                if m < KT - 1 or odd:
                    square(m, norm)

            def square(m, norm):
                if m >= 2:
                    act.wait_ge(sq_added, norm * KT + (m - 1))
                act.activation(sqt[:, m % 2, :], xT[:, m, :], ACT.Square).then_inc(sq_ready, 1)
            act.wait_ge(trig_arg, 1)
            for k in range(2):
                act.activation(sincos[:, k].rearrange("p t (r f) -> p t r f", f=HALF),
                               arg[:, k].unsqueeze(2).to_broadcast([P, TT, P // HALF, HALF]), ACT.Sin)\
                    .then_inc(sin_ready, 1)
            act.activation(rcol[:, TT:TT + 1], ones, ACT.Exp)
            for m in range(KT):
                if m < X_ACT:
                    wait_full(act, f"p{m}")
                    release(copy(xT[:, m, :], psum[:, PS.bank(f"p{m}"), :]), f"p{m}")
                wait_moved(act, f"p{m}")
                if m == 0:
                    wait_moved(act, "gain")
                prep(m, 0, params[:, m:m + 1])

            def ff_chunk(l, c, last):
                for m in range(KT):
                    wait_moved(act, f"f{m}", l, c)
                    act.activation(BH[:, m, :], relu[:, m % 2, :], ACT.Square).then_inc(bh_ready, 1)
                    if m % 2:
                        split_hi(U_FF + m // 2 + 2, l, (f"f{m}", l, c), c)
                for m in range(KT):
                    if last:
                        wait_moved(act, f"g{m}", l, c)
                        prep(m, l * 2 + 2, gl[:, G_NEXT + m:G_NEXT + m + 1])
                    if m % 2 and not (last and m // 2 >= 2):
                        split_hi(U_FF + 4 + m // 2 + 2, l, (f"g{m}", l, c), c)

            with act.Fori(0, DEPTH) as l:
                def queries_high(h):
                    rows = slice((h % 2) * DH, (h % 2) * DH + DH)
                    wait_moved(act, f"q{h // 2}", l)
                    copy(QS[h][rows, :], qT[rows, h // 2, :]).then_inc(qh_ready, 1)

                split_hi(0, l, None)
                split_hi(1, l, None)
                split_hi(2, l, ("cq1", l))
                wait_full(act, "nbc", l)
                release(copy(rs[:], psum[:, PS.bank("nbc"), :]), "nbc")
                split_hi(3, l, ("kr", l))
                for k, (src, name) in enumerate(((cq[:, 0, :], "cq0"), (cq[:, 1, :], "cq1"), (ckv[:], "ckv"))):
                    wait_moved(act, name, l)
                    act.activation(sqt[:, k, :], src, ACT.Square).then_inc(msq_ready, 1)
                split_hi(4, l, ("vc", l))
                wait_full(act, "gt", l)
                release(act.activation(gates[:].rearrange("p t g -> p (t g)"),
                                       psum[:, PS.bank("gt"), 0:TT * GATE_W], ACT.Exp, scale=-1.0), "gt")
                split_hi(5, l, ("kw", l))
                wait_moved(act, "ks", l)
                wait_moved(act, "kw", l)
                for g, half in ((0, 0), (1, 1), (0, 1), (1, 0)):
                    copy(KSH[half * DH:(half + 1) * DH, :, g, :], kraw[g * DH:(g + 1) * DH, :, :])\
                        .then_inc(kh_ready, 1)
                for t in range(TT):
                    wait_full(act, f"v{t}", l)
                    release(copy(VN[:, t, :], psum[:, PS.bank(f"v{t}"), 0:256], scale=rcol[:, t:t + 1]), f"v{t}")
                split_hi(6, l, ("v3", l))
                split_hi(7, l, ("q1", l))
                act.wait_ge(gelu_arg, l + 1)
                act.activation(hg[:], hg[:], ACT.Exp, scale=-2.0 * float(np.sqrt(2.0 / np.pi)))\
                   .then_inc(gelu_exp, 1)
                wait_full(act, "hv", l)
                for h in range(4):
                    queries_high(h)
                split_hi(8, l, ("q2", l))
                split_hi(9, l, ("u1", l))

                def up_q(h):
                    wait_full(act, f"uq{h}", l)
                    release(copy(QM[:, h, :], psum[:, PS.bank(f"uq{h}"), :]), f"uq{h}")

                for h in range(4):
                    up_q(h)
                for h in range(4, MLA_H):
                    up_q(h)
                act.wait_ge(csub_ready, l + 1)
                act.activation(sc[:], sc[:], ACT.Exp).then_inc(cexp_ready, 1)
                for p in range(3):
                    wait_full(act, f"kn{p}", l)
                    copy(KM[0:NOPE, 2 * p, :], psum[0:NOPE, PS.bank(f"kn{p}"), :])
                    release(copy(KM[0:NOPE, 2 * p + 1, :], psum[NOPE:P, PS.bank(f"kn{p}"), :]), f"kn{p}")
                for t in range(TT):
                    wait_full(act, f"vm{t}", l)
                    release(copy(VM[:, t, :], psum[:, PS.bank(f"vm{t}"), 0:MLA_H * VD]), f"vm{t}")

                for s in range(N_UNITS_ATT + 4):
                    if s == 2:
                        wait_full(act, "vm3", l)
                        queries_high(4)
                        queries_high(5)
                    if s == 1:
                        wait_full(act, "ct0", l)
                        release(copy(PTc[:, 0, :], psum[:, PS.bank("ct0"), :]), "ct0")
                    if s < N_UNITS_ATT:
                        scale = 1.0 if s < 2 * NSA_H else QK ** -0.5
                        for n, (i, b, col, pc) in enumerate(S_TILES):
                            if n < 2:
                                act.wait_ge(max_ready, l * 2 * N_UNITS_ATT + 2 * s + n + 1)
                            n = P * (i + 1)
                            e = act.activation(pr[s % 3][:, pc:pc + n], psum[:, b, col:col + n], ACT.Exp,
                                               bias=nms[:, s % 3, i:i + 1], scale=scale,
                                               accum_out=ssum[:, s % 3, i:i + 1])
                            if col or b != 1:
                                release(e, f"s{s}{'abc'[b]}")
                    if 2 <= s < N_UNITS_ATT + 2:
                        u = s - 2
                        wait_full(act, f"t{u}a", l)
                        release(copy(PT[:, u % 2, 0:512], psum[:, 3, :]), f"t{u}a")
                        wait_full(act, f"t{u}c", l)
                        release(copy(PT[:, u % 2, 1024:PW], psum[:, 5, 0:256]), f"t{u}c")
                    if s - 1 in POOL_AT:
                        k = POOL_AT.index(s - 1)
                        wait_full(act, f"py{k}", l)
                        copy(BH[:, 6 + k, :], psum[:, PS.bank(f"py{k}"), :], scale=gl[:, G_PS + k:G_PS + k + 1])\
                            .then_inc(bh_ready, 1)
                    u = s - 4
                    if u >= 0 and (u + 1 == N_UNITS_ATT or PAIR_OF[u + 1] != PAIR_OF[u]):
                        pair = PAIR_OF[u]
                        wait_full(act, f"o{pair}", l)
                        copy(BH[:, pair, :], psum[:, PS.bank(f"o{pair}"), :]).then_inc(bh_ready, 1)
                for m in range(KT):
                    wait_moved(act, f"x{m}", l)
                    prep(m, l * 2 + 1, gl[:, G_LN2 + m:G_LN2 + m + 1], odd=True)
                    if m % 2:
                        split_hi(U_OUT + m // 2 + 2, l, (f"x{m}", l))
                wait_full(act, "nbc2", l)
                release(copy(rs[:], psum[:, PS.bank("nbc2"), :]), "nbc2")
                with act.Fori(0, CHUNKS - 1) as c:
                    ff_chunk(l, c, False)
                copy(identr[:], ident).then_inc(identr_ready, 1)
                ff_chunk(l, CHUNKS - 1, True)

            square(KT - 1, 2 * DEPTH)
            act.wait_ge(rcol_ready, 2 * DEPTH + 1)
            for t in range(TT):
                n = 2 * t
                wait_full(act, f"y{n}")
                copy(io[:, t, 0:512], psum[:, PS.bank(f"y{n}"), :], scale=rcol[:, t:t + 1]).then_inc(y_act, 1)

        @block.gpsimd
        def _(pool):
            chain = Chain(pool, pool_step, POOL_PL)

            def copy(o, i, r=slice(0, P)):
                one = ct[r, K_ONE:K_ONE + 1]
                for _ in i.shape[2:]:
                    one = one.unsqueeze(1)
                return pool.tensor_tensor(o, i, one.to_broadcast(list(i.shape)), ALU.mult)

            pool.memset(KB[:], 0.0)
            pool.memset(pw[:], 0.0).then_inc(zeros_set, 1)
            pool.memset(kcv[:, :, T:], 0.0).then_inc(w_hi, 1)
            pool.memset(up[:, :, 0:CMP_STRIDE], 0.0).then_inc(w_lo, 1)
            pool.wait_ge(const_loaded, 48)
            pool.tensor_copy(identb[:], ident).then_inc(masks_set, 1)
            pool.tensor_copy(trib[:], trif[:]).then_inc(masks_set, 1)

            def split_lo(n, l, c=None):
                pool.wait_ge(*split_counts(n, l, 0 if c is None else c)[0])
                w = IN_WIDTH[n] if n < U_OUT else 256
                s, a = n % 2, P if n == 0 else 0
                pool.tensor_tensor(WL[:, s, :, a:w], raw[:, s, :, a:w], f32(WH[:, s, :, a:w]), ALU.subtract)\
                    .then_inc(w_lo, 1)

            def add_square(m, norm):
                pool.wait_ge(sq_ready, norm * KT + (m + 1))
                if m == 0:
                    copy(rs[:], sqt[:, 0, :]).then_inc(sq_added, 1)
                else:
                    pool.wait_ge(sq_added, norm * KT + m)
                    pool.tensor_tensor(rs[:], rs[:], sqt[:, m % 2, :], ALU.add).then_inc(sq_added, 1)

            for m in range(KT):
                add_square(m, 0)

            def ff_chunk(l, c, last):
                for m in range(KT):
                    wait_moved(pool, f"f{m}", l, c)
                    pool.tensor_tensor(asq[:, m % 2, :], relu[:, m % 2, :], relu[:, m % 2, :], ALU.mult)\
                        .then_inc(asq_ready, 1)
                    if m % 2:
                        split_lo(U_FF + m // 2 + 2, l, c)
                for m in range(KT):
                    if last:
                        add_square(m, l * 2 + 2)
                    if m % 2 and not (last and m // 2 >= 2):
                        split_lo(U_FF + 4 + m // 2 + 2, l, c)

            with pool.Fori(0, DEPTH) as l:
                chain.layer(l)
                split_lo(0, l)
                pool.wait_ge(raw_loaded[1], l * (16 * RAW_PL[1]) + 16 * raw_count(1))
                kr = raw[:, 1, :, 192:256]
                copy(kr[:, :, 32:48], kr[:, :, 16:32]).then_inc(kr_cols, 1)
                copy(kr[:, :, 48:64], kr[:, :, 0:16]).then_inc(kr_cols, 1)
                split_lo(1, l)
                pool.wait_ge(small_loaded, (l + 1) * (16 * NSMALL))
                for g in range(2):
                    copy(wq[:, g, :, QK:QK + 16], wq[:, g, :, QK - 16:QK])
                    copy(wq[:, g, :, QK + 16:P], wq[:, g, :, NOPE:NOPE + 16]).then_inc(wq_cols, 1)
                split_lo(2, l)
                split_lo(3, l)
                pool.wait_ge(krot_ready, l + 1)
                pool.wait_ge(*split_counts(3, l)[1])
                chain.link(pool.tensor_tensor(krt[64:96, :], krt[64:96, :], krz[64:96, :], ALU.add))
                for n in range(4, 9):
                    split_lo(n, l)
                E = T + CMP_STRIDE
                for k in range(2):
                    wait_moved(pool, f"u{k}", l)
                    chain.link(pool.tensor_tensor(pa[:, k, 2:E], up[:, k, 2:E], up[:, k, 1:E - 1], ALU.add))
                    last = pool.tensor_tensor(pb[:, k, 4:E], pa[:, k, 4:E], pa[:, k, 2:E - 2], ALU.add)
                    if k:
                        chain.link(last)
                        chain.link(pool.tensor_tensor(pa[:, k, 8:E], pb[:, k, 8:E], pb[:, k, 4:E - 4], ALU.add))
                        last = pool.tensor_tensor(pb[64:P, k, 16:E], pa[64:P, k, 16:E], pa[64:P, k, 8:E - 8], ALU.add)
                    last.then_inc(pool_add, 1)
                pool.wait_ge(pool_add, l * 2 + 2)
                split_lo(9, l)
                pool.wait_ge(*split_counts(9, l)[1])
                copy(KM[64:96, :, :], krt[64:96, :].unsqueeze(1).to_broadcast([32, MLA_H, T]), slice(64, 96))\
                    .then_inc(kr_spread, 1)
                pool.wait_ge(kr_spread, l + 1)
                for u in range(N_UNITS_ATT):
                    for k, (i, _, _, pc) in enumerate(S_TILES):
                        if k < 2:
                            pool.wait_ge(fac_ready, l * 2 * N_UNITS_ATT + 2 * u + k + 1)
                        n = P * (i + 1)
                        p = pr[u % 3][:, pc:pc + n]
                        pool.tensor_tensor(p, p, fac[:, u % 3, i:i + 1].to_broadcast([P, n]), ALU.mult)\
                            .then_inc(p_ready, 1)
                    if u in ROTATE_AT:
                        h = ROTATE_AT.index(u)
                        a, b = rot(h)
                        pool.wait_ge(p_ready, l * 4 * N_UNITS_ATT + 4 * (u + 1))
                        pool.wait_ge(qrot_ready, l * MLA_H + h + 1)
                        pool.tensor_tensor(QM[64:96, h, :], a, b, ALU.add).then_inc(qm_ready, 1)
                        pool.wait_ge(qm_ready, l * MLA_H + h + 1)
                for m in range(KT):
                    add_square(m, l * 2 + 1)
                    if m % 2:
                        split_lo(U_OUT + m // 2 + 2, l)
                with pool.Fori(0, CHUNKS - 1) as c:
                    ff_chunk(l, c, False)
                ff_chunk(l, CHUNKS - 1, True)
                assert chain.n == POOL_PL, chain.n

        @block.vector
        def _(dve):
            chain = Chain(dve, dve_step, DVE_PL, DVE_PRE)

            def bank(name):
                return psum[:, PS.bank(name), :]

            def low(m, gain, need):
                dve.wait_ge(xh_ready, need)
                dve.scalar_tensor_tensor(out=XL[:, m, :], in0=xT[:, m, :], scalar=gain, in1=f32(XH[:, m, :]),
                                         op0=ALU.mult, op1=ALU.subtract).then_inc(xl_ready, 1)

            def rsqrt(n, o, ready):
                a, t, y = na[:, 0:n], nt[:, 0:n], ni[:, 0:n]
                chain.link(dve.tensor_scalar(y, a.bitcast(I32), 1, None, ALU.logical_shift_right))
                chain.link(dve.tensor_scalar(y, y, -1.0, float(0x5f3759df), ALU.mult, ALU.add))
                y = y.bitcast(F32)
                for k in range(3):
                    chain.link(dve.tensor_tensor(t, y, y, ALU.mult))
                    chain.link(dve.tensor_tensor(t, t, a, ALU.mult))
                    chain.link(dve.tensor_scalar(t, t, -0.5, 1.5, ALU.mult, ALU.add))
                    if k < 2:
                        chain.link(dve.tensor_tensor(y, y, t, ALU.mult))
                dve.tensor_tensor(o, y, t, ALU.mult).then_inc(*ready)

            def residual_norm(name, norm, spread, l=0):
                wait_full(dve, name, l)
                release(dve.tensor_scalar(na[:, 0:TT], bank(name)[:, 0:TT], 1.0 / D, EPS, ALU.mult, ALU.add), name)
                wait_moved(dve, name, l)
                rsqrt(TT, rcol[:, 0:TT], (rcol_ready, 1))
                dve.wait_ge(rcol_ready, norm + 1)
                if spread:
                    for t in range(TT):
                        d = dve.tensor_scalar(sqt[:, 0, t * P:(t + 1) * P], ident, rcol[:, t:t + 1], None, ALU.mult)
                    d.then_inc(diag_ready, 1)

            dve.wait_ge(const_loaded, 48)
            chain.base, two_pi = 0, 2.0 * np.pi
            c1 = 6.28125
            c2 = float(np.float32(two_pi - c1).view(np.uint32) & np.uint32(0xfffff000))
            c2 = float(np.uint32(c2).view(np.float32))
            c3 = float(np.float32(two_pi - c1 - c2))
            flat = [t[:].rearrange("p s t f -> p s (t f)") for t in (ang, turns, arg)]
            fa, ft, fr = flat[0].to_broadcast([P, 2, TT * HALF]), flat[1], flat[2]
            chain.link(dve.tensor_copy(posf[:], posi[:]))
            chain.link(dve.tensor_tensor(ang[:, 0], posf[:].unsqueeze(2).to_broadcast([P, TT, HALF]),
                                         ct[:, K_INVF:K_INVF + HALF].unsqueeze(1).to_broadcast([P, TT, HALF]), ALU.mult))
            for k, quarter in ((0, 0.0), (1, 0.25)):
                d = dve.tensor_scalar(ft[:, k], flat[0][:, 0], float(1.0 / two_pi), quarter, ALU.mult, ALU.add)
            chain.link(d)
            chain.link(dve.tensor_scalar(ft, ft, ROUND, -ROUND, ALU.add, ALU.add))
            chain.link(dve.scalar_tensor_tensor(out=fr, in0=ft, scalar=-c1, in1=fa, op0=ALU.mult, op1=ALU.add))
            chain.link(dve.scalar_tensor_tensor(out=fr, in0=ft, scalar=-c2, in1=fr, op0=ALU.mult, op1=ALU.add))
            chain.link(dve.scalar_tensor_tensor(out=fr, in0=ft, scalar=-c3, in1=fr, op0=ALU.mult, op1=ALU.add))
            chain.link(dve.tensor_scalar(fr[:, 1], fr[:, 1], float(0.5 * np.pi), None, ALU.add))
            dve.tensor_scalar(fr, fr, 3.1415925, -3.1415925, ALU.min, ALU.max).then_inc(trig_arg, 1)
            n = PAR0 + DEPTH * PAR_L
            def in_order(t):
                return t.rearrange("p (q t) -> p q t", t=TT)

            def by_token(name):
                return bank(name).rearrange("p (t q) -> p q t", t=TT)

            wait_full(dve, "gain")
            release(dve.tensor_copy(params[:, 0:PAR0], bank("gain")[:, 0:PAR0]), "gain")
            def moved_in(m):
                wait_full(dve, f"p{m}")
                release(dve.tensor_copy(xT[:, m, :], bank(f"p{m}")), f"p{m}")

            for m in range(KT):
                if m == 1:
                    wait_full(dve, "sin")
                    release(dve.tensor_scalar(in_order(sintab[:]), by_token("sin"), ct[:, K_SIGN:K_SIGN + 1], None,
                                              ALU.mult), "sin")
                if m == 2:
                    wait_full(dve, "cos")
                    release(dve.tensor_copy(in_order(costab[:]), by_token("cos")), "cos")
                if m + 1 >= X_ACT and m + 1 < KT:
                    moved_in(m + 1)
                wait_moved(dve, f"p{m}")
                low(m, params[:, m:m + 1], m + 1)
            wait_full(dve, "par")
            release(dve.tensor_copy(params[:, PAR0:n], bank("par")[:, PAR0:n]), "par")
            wait_moved(dve, "par")
            assert chain.n == DVE_PRE, chain.n
            chain.base = DVE_PRE
            dve.wait_ge(w_hi, 1)
            dve.wait_ge(w_lo, 1)
            dve.wait_ge(zeros_set, 1)

            def ff_chunk(l, c, last):
                for m in range(KT):
                    wait_full(dve, f"f{m}", l, c)
                    release(dve.scalar_tensor_tensor(out=relu[:, m % 2, :], in0=bank(f"f{m}"), scalar=0.0, in1=rs[:],
                                                     op0=ALU.max, op1=ALU.mult), f"f{m}")
                    dve.wait_ge(bh_ready, l * B_PL + c * KT + (KT + m + 1))
                    dve.wait_ge(asq_ready, l * (KT * CHUNKS) + c * KT + (m + 1))
                    dve.tensor_tensor(BL[:, m, :], asq[:, m % 2, :], f32(BH[:, m, :]), ALU.subtract)\
                       .then_inc(bl_ready, 1)
                for m in range(KT):
                    wait_full(dve, f"g{m}", l, c)
                    release(dve.tensor_tensor(xT[:, m, :], bank(f"g{m}"), xT[:, m, :], ALU.add), f"g{m}")
                    if last:
                        low(m, gl[:, G_NEXT + m:G_NEXT + m + 1], l * 2 * KT + (2 * KT + m + 1))

            with dve.Fori(0, DEPTH) as l:
                chain.layer(l)
                for n in range(2):
                    dve.wait_ge(w_hi, l * HI_PL + n + 2)
                    k = slice(n * KT // 2, (n + 1) * KT // 2)
                    dve.tensor_tensor(WL[:, 0, k, 0:P], raw[:, 0, k, 0:P], f32(WH[:, 0, k, 0:P]), ALU.subtract)\
                        .then_inc(w_lo0, 1)
                plain_waits(dve, (xl_ready, (l * 2 + 1) * KT))
                dve.tensor_copy(gl[:], params[:, bass.ds(l * PAR_L + PAR0, PAR_L)]).then_inc(gl_ready, 1)
                dve.wait_ge(gl_ready, l + 1)
                residual_norm("ncol", l * 2, True, l)
                wait_full(dve, "post", l)
                release(dve.tensor_copy(pos2[:], bank("post")[:, 0:2 * CMP_LEN]), "post")
                wait_moved(dve, "nbc", l)

                def scaled(name, o):
                    wait_full(dve, name, l)
                    release(dve.tensor_tensor(o, bank(name), rs[:], ALU.mult), name)

                def queries(k):
                    name = f"q{k}"
                    wait_full(dve, name, l)
                    release(dve.scalar_tensor_tensor(out=qT[:, k, :], in0=bank(name), scalar=DH ** -0.5, in1=rs[:],
                                                     op0=ALU.mult, op1=ALU.mult), name)

                def queries_low(h):
                    r = (h % 2) * DH
                    dve.wait_ge(qh_ready, l * NSA_H + h + 1)
                    dve.tensor_tensor(QS[h][DH - r:2 * DH - r, :], qT[r:r + DH, h // 2, :], f32(QS[h][r:r + DH, :]),
                                      ALU.subtract).then_inc(ql_ready, 1)

                scaled("cq0", cq[:, 0, :])
                scaled("cq1", cq[:, 1, :])
                scaled("ckv", ckv[:])
                scaled("kr", krz[:])
                wait_moved(dve, "kr", l)
                chain.link(dve.tensor_tensor(krt[64:96, :], krz[64:96, :], costab[64:96, :], ALU.mult))
                dve.tensor_tensor(krz[64:96, :], krz[96:128, :], sintab[96:128, :], ALU.mult).then_inc(krot_ready, 1)
                scaled("kc", kcv[:, 0, 0:T])
                scaled("vc", kcv[:, 1, 0:T])
                wait_full(dve, "mcol", l)
                chain.link(dve.tensor_scalar(na[:, 0:TT], bank("mcol")[:, 0:TT], 1.0 / Q_LORA, EPS, ALU.mult, ALU.add))
                release(dve.tensor_scalar(na[:, TT:2 * TT], bank("mcol")[:, TT:2 * TT], 1.0 / KV_LORA, EPS,
                                          ALU.mult, ALU.add), "mcol")
                wait_moved(dve, "mcol", l)
                rsqrt(2 * TT, rcol[:, TT:3 * TT], (dve_step, 1))
                chain.n += 1
                dve.wait_ge(dve_step, l * DVE_PL + (DVE_PRE + chain.n))
                for t in range(2 * TT):
                    d = dve.tensor_scalar(sqt[:, 1 + t // TT, (t % TT) * P:(t % TT + 1) * P], ident,
                                          rcol[:, TT + t:TT + t + 1], None, ALU.mult)
                d.then_inc(mdiag_ready, 1)
                scaled("ks", kraw[:, 0, :])
                scaled("kw", kraw[:, 1, :])
                wait_full(dve, "mbq", l)
                for k in range(2):
                    d = dve.scalar_tensor_tensor(out=cq[:, k, :], in0=cq[:, k, :], scalar=gl[:, G_QN + k:G_QN + k + 1],
                                                 in1=bank("mbq"), op0=ALU.mult, op1=ALU.mult)
                release(d, "mbq")
                wait_full(dve, "mbk", l)
                release(dve.scalar_tensor_tensor(out=ckv[:], in0=ckv[:], scalar=gl[:, G_KVN:G_KVN + 1],
                                                 in1=bank("mbk"), op0=ALU.mult, op1=ALU.mult), "mbk")
                wait_moved(dve, "post", l)
                wait_moved(dve, "vc", l)
                for v in range(2):
                    for par in range(2):
                        for g in range(2):
                            src = kcv[g * DH:(g + 1) * DH, v, :]
                            rows = src.ap[0]
                            win = bass.AP(tensor=src.tensor, offset=src.offset + par,
                                          ap=[rows, [2, 16], [CMP_STRIDE, NB]])
                            pos = pos2[g * DH:(g + 1) * DH, v * CMP_LEN + par:(v + 1) * CMP_LEN:2]
                            dve.tensor_tensor(bcmp[par * DH:(par + 1) * DH, v, :, g * NB:(g + 1) * NB], win,
                                              pos.unsqueeze(2).to_broadcast([DH, 16, NB]), ALU.add)\
                               .then_inc(bcmp_ready, 1)
                wait_moved(dve, "gt", l)
                chain.link(dve.tensor_scalar(gates[:], gates[:], 1.0, None, ALU.add))
                dve.reciprocal(gates[:], gates[:]).then_inc(gates_ready, 1)
                queries(0)
                queries(1)
                wait_full(dve, "hk", l)
                release(dve.tensor_copy(hx[:, 0, :], bank("hk")[0:DH, 0:2 * NB]), "hk")
                wait_full(dve, "hv", l)
                release(dve.tensor_copy(hx[:, 1, :], bank("hv")[0:DH, 0:2 * NB]), "hv")
                wait_moved(dve, "hk", l)
                wait_moved(dve, "hv", l)
                chain.link(dve.tensor_tensor(hg[:], hx[:], hx[:], ALU.mult))
                chain.link(dve.tensor_scalar(hg[:], hg[:], 0.044715, 1.0, ALU.mult, ALU.add))
                dve.tensor_tensor(hg[:], hg[:], hx[:], ALU.mult).then_inc(gelu_arg, 1)
                queries(2)
                dve.wait_ge(gelu_exp, l + 1)
                chain.link(dve.tensor_scalar(hg[:], hg[:], 1.0, None, ALU.add))
                chain.link(dve.reciprocal(hg[:], hg[:]))
                dve.tensor_tensor(hg[:], hg[:], hx[:], ALU.mult).then_inc(hg_ready, 1)
                for h in range(4):
                    queries_low(h)
                scaled("u0", up[:, 0, CMP_STRIDE:])
                scaled("u1", up[:, 1, CMP_STRIDE:])
                def rotate(h):
                    wait_moved(dve, f"uq{h}", l)
                    if h >= 2:
                        dve.wait_ge(qm_ready, l * MLA_H + h - 1)
                    a, b = rot(h)
                    chain.link(dve.tensor_tensor(a, QM[64:96, h, :], costab[64:96, :], ALU.mult))
                    dve.tensor_tensor(b, QM[96:128, h, :], sintab[96:128, :], ALU.mult).then_inc(qrot_ready, 1)

                wait_full(dve, "k2", l)
                for half in range(2):
                    rows = slice(half * DH, (half + 1) * DH)
                    for g in range(NSA_G):
                        ps = [q for q in range(NSA_H // 2) if (2 * q + half) // NSA_HPG == g]
                        src = bank("k2")[rows, g * NB:(g + 1) * NB].unsqueeze(1).to_broadcast([DH, len(ps), NB])
                        d = dve.tensor_copy(KB[rows, ps[0]:ps[-1] + 1, half * NB:(half + 1) * NB], src)
                release(d, "k2")
                wait_full(dve, "w2", l)
                dve.tensor_copy(vcr[:, 0, :], bank("w2")[:, 0:DH])
                release(dve.tensor_copy(vcr[0:2 * NB, 1, :], bank("w2")[0:2 * NB, DH:2 * DH]), "w2")
                for b in range(2):
                    wait_full(dve, f"cs{b}", l)
                    for t in range(2 * b, 2 * b + 2):
                        w = NSA_H * NB
                        d = dve.scalar_tensor_tensor(
                            out=sc[:, t, :, :],
                            in0=bank(f"cs{b}")[:, (t % 2) * w:(t % 2 + 1) * w].rearrange("p (h n) -> p h n", n=NB),
                            scalar=1.0,
                            in1=ct[:, K_CM + t * NB:K_CM + (t + 1) * NB].unsqueeze(1).to_broadcast([P, NSA_H, NB]),
                            op0=ALU.mult, op1=ALU.add)
                    release(d, f"cs{b}")
                scv = sc[:].rearrange("p t h n -> p (t h) n")
                wait_moved(dve, "cs0", l)
                wait_moved(dve, "cs1", l)
                chain.link(dve.tensor_reduce(cmx[:], scv, AX_X, ALU.max))
                chain.link(dve.tensor_scalar(cmx[:], cmx[:], NEG_GUARD, None, ALU.max))
                dve.tensor_tensor(scv, scv, cmx[:].unsqueeze(2).to_broadcast([P, TT * NSA_H, NB]), ALU.subtract)\
                   .then_inc(csub_ready, 1)
                dve.wait_ge(kh_ready, l * 4 + 2)
                for g in range(2):
                    rows = slice(g * DH, (g + 1) * DH)
                    for br in range(2):
                        dve.tensor_tensor(KSL[br][rows, g, :], kraw[rows, br, :], f32(KSH[rows, br, g, :]), ALU.subtract)\
                           .then_inc(kl_ready, 1)
                for g in range(2):
                    for br in range(2):
                        if br == 0:
                            dve.wait_ge(kl_ready, l * 8 + 2 * g + 2)
                        dve.tensor_copy(KSL[br][(1 - g) * DH:(2 - g) * DH, g, :], KSL[br][g * DH:(g + 1) * DH, g, :])\
                           .then_inc(kl_ready, 1)

                dve.wait_ge(cexp_ready, l + 1)
                chain.link(dve.tensor_reduce(csm[:], scv, AX_X, ALU.add))
                chain.link(dve.tensor_scalar(csm[:], csm[:], TINY, None, ALU.max))
                chain.link(dve.reciprocal(csm[:], csm[:]))
                dve.wait_ge(gates_ready, l + 1)
                csv = csm[:].rearrange("p (t h) -> p t h", t=TT)
                chain.link(dve.tensor_tensor(csv, csv, gates[:, :, 0:GATE_W:3], ALU.mult))
                dve.tensor_tensor(scv, scv, csm[:].unsqueeze(2).to_broadcast([P, TT * NSA_H, NB]), ALU.mult)\
                   .then_inc(cp_ready, 1)
                def pooled(k):
                    dve.wait_ge(pool_add, l * 2 + k + 1)
                    for half, s in ((0, pa), (1, pb)):
                        r = slice(half * 64, half * 64 + 64)
                        head, rest = slice(CMP_STRIDE, 2 * CMP_STRIDE), slice(2 * CMP_STRIDE, T + CMP_STRIDE)
                        rc = ct[r, K_RC + k * 16:K_RC + (k + 1) * 16]
                        chain.link(dve.tensor_tensor(pb[r, k, 0:CMP_STRIDE], s[r, k, head], rc, ALU.mult))
                        dve.tensor_tensor(pb[r, k, head], pb[r, k, 0:CMP_STRIDE], up[r, k, head], ALU.subtract)
                        d = dve.scalar_tensor_tensor(out=pb[r, k, rest], in0=s[r, k, rest],
                                                     scalar=ct[r, K_INVW + k:K_INVW + k + 1], in1=up[r, k, rest],
                                                     op0=ALU.mult, op1=ALU.subtract)
                    d.then_inc(pooled_ready, 1)

                def transposed(u):
                    wait_full(dve, f"t{u}b", l)
                    release(dve.tensor_copy(PT[:, u % 2, 512:1024], psum[:, 4, :]), f"t{u}b")

                def maxima(u, banks):
                    nsa, k = u < 2 * NSA_H, u % 3
                    tiles = [t for t in S_TILES if "abc"[t[1]] in banks]
                    for i, b, col, _ in tiles:
                        if col == 0:
                            wait_full(dve, f"s{u}{'abc'[b]}", l)
                        d = dve.tensor_reduce((nms if nsa else nmax)[:, k, i:i + 1], psum[:, b, col:col + P * (i + 1)],
                                              AX_X, ALU.max, negate=True)
                    if not nsa:
                        chain.link(d)
                        part = S_PART[banks]
                        d = dve.tensor_scalar(nms[:, k, part], nmax[:, k, part], QK ** -0.5, None, ALU.mult)
                    d.then_inc(max_ready, 1)

                def factors(u, banks):
                    k, part = u % 3, S_PART[banks]
                    wait_moved(dve, f"s{u}{banks[-1]}", l)
                    d = dve.reciprocal(fac[:, k, part], ssum[:, k, part])
                    if u < 2 * NSA_H:
                        chain.link(d)
                        col = 3 * UNIT[u][0] + 1 + UNIT[u][1]
                        d = dve.tensor_tensor(fac[:, k, part], fac[:, k, part], gates[:, part, col], ALU.mult)
                    d.then_inc(fac_ready, 1)

                for s in range(N_UNITS_ATT + 4):
                    if s < N_UNITS_ATT:
                        maxima(s, "a")
                    if 1 <= s <= N_UNITS_ATT:
                        factors(s - 1, "bc")
                    if s < N_UNITS_ATT:
                        maxima(s, "bc")
                    if s == 2:
                        queries_low(4)
                        queries_low(5)
                    if s == 1:
                        wait_full(dve, "ct1", l)
                        release(dve.tensor_copy(PTc[0:2 * NB, 1, :], bank("ct1")[0:2 * NB, :]), "ct1")
                    if s < N_UNITS_ATT:
                        factors(s, "a")
                    if s < 2:
                        pooled(s)
                    if 2 <= s < N_UNITS_ATT + 2:
                        transposed(s - 2)
                    if s in ROTATE_AT:
                        rotate(ROTATE_AT.index(s))
                    if s - 1 in POOL_AT:
                        k = POOL_AT.index(s - 1)
                        dve.wait_ge(bh_ready, l * B_PL + k + 1)
                        release(dve.scalar_tensor_tensor(out=BL[:, 6 + k, :], in0=bank(f"py{k}"),
                                                         scalar=gl[:, G_PS + k:G_PS + k + 1], in1=f32(BH[:, 6 + k, :]),
                                                         op0=ALU.mult, op1=ALU.subtract), f"py{k}")
                    u = s - 4
                    if u >= 0 and (u + 1 == N_UNITS_ATT or PAIR_OF[u + 1] != PAIR_OF[u]):
                        pair = PAIR_OF[u]
                        dve.wait_ge(bh_ready, l * B_PL + 3 + pair)
                        release(dve.tensor_tensor(BL[:, pair, :], bank(f"o{pair}"), f32(BH[:, pair, :]), ALU.subtract),
                                f"o{pair}")
                for m in range(KT):
                    wait_full(dve, f"x{m}", l)
                    release(dve.tensor_tensor(xT[:, m, :], bank(f"x{m}"), xT[:, m, :], ALU.add), f"x{m}")
                    low(m, gl[:, G_LN2 + m:G_LN2 + m + 1], l * 2 * KT + (KT + m + 1))
                residual_norm("ncol2", l * 2 + 1, True, l)
                plain_waits(dve, (moved[PS.bank("nbc2")], PS.before("nbc2", l) + 1))
                with dve.Fori(0, CHUNKS - 1) as c:
                    ff_chunk(l, c, False)
                ff_chunk(l, CHUNKS - 1, True)
                assert chain.n == DVE_PL, chain.n
            chain.layer(DEPTH)
            residual_norm("ncol3", 2 * DEPTH, False)
            for t in range(TT):
                n = 2 * t + 1
                wait_full(dve, f"y{n}")
                dve.tensor_scalar(io[:, t, 512:1024], bank(f"y{n}"), rcol[:, t:t + 1], None, ALU.mult)\
                   .then_inc(y_dve, 1)


def tables():
    c = np.zeros((P, K_W), np.float32)
    p = np.arange(P)
    c[:, K_ID:K_ID + P] = np.eye(P)
    for t in range(TT):
        q = t * P + p
        end = np.arange(NB) * CMP_STRIDE + CMP_LEN - 1
        valid = (end[None, :] <= q[:, None]) & (np.arange(NB)[None, :] < NB - 1)
        c[:, K_CM + t * NB:K_CM + (t + 1) * NB] = np.where(valid, 0.0, NEG)
    for k in range(2):
        for half in range(2):
            w = 2 ** (1 + 2 * k + half)
            rows = slice(half * 64, half * 64 + 64)
            c[rows, K_RC + k * 16:K_RC + (k + 1) * 16] = 1.0 / np.minimum(np.arange(16) + 1, w)
            c[rows, K_INVW + k] = 1.0 / w
    half = ROPE // 2
    inv = np.power(np.float32(10000.0), -(np.arange(half, dtype=np.float32) / np.float32(half)))
    c[:, K_INVF:K_INVF + half] = inv
    c[:, K_SIGN] = np.where(p % ROPE < half, -1.0, 1.0)
    c[:, K_ONE] = 1.0
    tri = np.where(p[None, :] <= p[:, None], 0.0, NEG).astype(np.float32)
    return c, tri


_INS = ["x", "positions", "ln1_g", "w_in", "nsa_cmp_pos", "nsa_cmp_w1", "nsa_cmp_w2", "mla_q_norm", "mla_w_qup",
        "mla_kv_norm", "mla_w_kvup", "pool_w", "pool_scale", "w_out", "ln2_g", "w_ff1", "w_ff2", "final_g"]


def kernel(**inputs):
    import concourse.bacc as _bacc
    from concourse.bass_utils import run_bass_kernel_spmd as _run

    nc = _bacc.Bacc("TRN2", target_bir_lowering=False, num_devices=1)
    arrays = {n: np.ascontiguousarray(inputs[n]) for n in _INS}
    arrays["consts"], arrays["tri"] = tables()
    args = [nc.dram_tensor(f"in_{n}", a.shape, mybir.dt.from_np(a.dtype), kind="ExternalInput").ap()
            for n, a in arrays.items()]
    out = nc.dram_tensor("out_0", (1, T, D), F32, kind="ExternalOutput").ap()
    build(nc, *args, out)
    r = _run(nc, [{f"in_{n}": a for n, a in arrays.items()}], core_ids=[0])
    return r.results[0]["out_0"]
```
